# Optimizing a Trainium2 kernel written in Bass

```python
import jax, jax.numpy as jnp
from jax import lax
import numpy as np

D_MODEL = 2048
BATCH = 1
SEQ = 512
DEPTH = 1

BLOCK = 128
ROPE_THETA = 10000.0
LN_EPS = 1e-5
A_HEADS = 16
A_KV_HEADS = 2
A_GROUP = A_HEADS // A_KV_HEADS
A_HEAD_DIM = 64
A_WINDOW = 128
A_WIDTH = A_HEADS * A_HEAD_DIM
A_KV_WIDTH = A_KV_HEADS * A_HEAD_DIM
B_PATTERNS = ((128, 1), (512, 4), (2048, 16))
B_N_GROUPS = len(B_PATTERNS)
B_HEADS_PER_GROUP = 4
B_HEAD_DIM = 128
B_GROUP_WIDTH = B_HEADS_PER_GROUP * B_HEAD_DIM
B_QKV_WIDTH = B_N_GROUPS * B_GROUP_WIDTH
B_OUT_WIDTH = B_GROUP_WIDTH
N_BRANCHES = 2
IN_SIZES = (A_WIDTH, A_KV_WIDTH, A_KV_WIDTH, A_WIDTH,
            B_QKV_WIDTH, B_QKV_WIDTH, B_QKV_WIDTH, B_OUT_WIDTH,
            D_MODEL, D_MODEL)
D_IN = sum(IN_SIZES)
IN_OFFSETS = tuple(int(o) for o in np.cumsum(IN_SIZES)[:-1])
DN_ALPHA = float((2 * DEPTH) ** 0.25)
DN_BETA = float((8 * DEPTH) ** -0.25)

kernel_name = "hybrid_swa_sink_dilated_gated_deepnorm"

def apply_rope(t, positions):
    half = t.shape[-1] // 2
    inv_freq = ROPE_THETA ** (-jnp.arange(half, dtype=jnp.float32) / half)
    ang = positions.astype(jnp.float32)[..., None] * inv_freq
    cos = jnp.cos(ang)[:, :, None, :]
    sin = jnp.sin(ang)[:, :, None, :]
    t1 = t[..., :half].astype(jnp.float32)
    t2 = t[..., half:].astype(jnp.float32)
    out = jnp.concatenate([t1 * cos - t2 * sin, t2 * cos + t1 * sin], axis=-1)
    return out.astype(t.dtype)

def pad_seq(t):
    pad = (-t.shape[1]) % BLOCK
    return jnp.pad(t, [(0, 0), (0, pad)] + [(0, 0)] * (t.ndim - 2))

def banded_attention(q, k, v, max_dist, sink=None):
    n, L, kvh, g, dh = q.shape
    nb = L // BLOCK
    qb = q.reshape(n, nb, BLOCK, kvh, g, dh)
    kb = k.reshape(n, nb, BLOCK, kvh, dh)
    vb = v.reshape(n, nb, BLOCK, kvh, dh)
    zero_blk = ((0, 0), (1, 0), (0, 0), (0, 0), (0, 0))
    kk = jnp.concatenate([jnp.pad(kb, zero_blk)[:, :-1], kb], axis=2)
    vv = jnp.concatenate([jnp.pad(vb, zero_blk)[:, :-1], vb], axis=2)
    s = jnp.einsum('ncqhgd,nckhd->nchgqk', qb, kk,
                   preferred_element_type=jnp.float32) * (dh ** -0.5)
    q_idx = jnp.arange(BLOCK)[:, None] + BLOCK
    k_idx = jnp.arange(2 * BLOCK)[None, :]
    dist = q_idx - k_idx
    band = (dist >= 0) & (dist <= max_dist)
    key_pos = jnp.arange(nb)[:, None] * BLOCK - BLOCK + jnp.arange(2 * BLOCK)[None, :]
    mask = band[None] & (key_pos >= 0)[:, None, :]
    s = jnp.where(mask[None, :, None, None], s, -jnp.inf)
    m = jnp.max(s, axis=-1)
    if sink is not None:
        sk = sink.astype(jnp.float32)[None, None, :, :, None]
        m = jnp.maximum(m, sk)
    p = jnp.exp(s - m[..., None])
    denom = jnp.sum(p, axis=-1)
    if sink is not None:
        denom = denom + jnp.exp(sk - m)
    o = jnp.einsum('nchgqk,nckhd->ncqhgd', p, vv.astype(jnp.float32))
    denom_t = denom.transpose(0, 1, 4, 2, 3)
    o = o / denom_t[..., None]
    lse = (m.transpose(0, 1, 4, 2, 3) + jnp.log(denom_t)).reshape(n, L, kvh, g)
    return o.reshape(n, L, kvh, g, dh), lse

def dilated_group(q, k, v, window, dilation):
    bn, s_len, h, dh = q.shape
    L = s_len // dilation

    def to_sub(t):
        return t.reshape(bn, L, dilation, h, dh).transpose(0, 2, 1, 3, 4).reshape(bn * dilation, L, h, dh)

    qs, ks, vs = pad_seq(to_sub(q)), pad_seq(to_sub(k)), pad_seq(to_sub(v))
    o, lse = banded_attention(qs[:, :, :, None, :], ks, vs, window // dilation)
    o = o[:, :L, :, 0].reshape(bn, dilation, L, h, dh).transpose(0, 2, 1, 3, 4).reshape(bn, s_len, h, dh)
    lse = lse[:, :L, :, 0].reshape(bn, dilation, L, h).transpose(0, 2, 1, 3).reshape(bn, s_len, h)
    return o, lse

def layer_norm(z, g, b):
    z = z.astype(jnp.float32)
    mu = jnp.mean(z, axis=-1, keepdims=True)
    var = jnp.mean(jnp.square(z - mu), axis=-1, keepdims=True)
    return (z - mu) * lax.rsqrt(var + LN_EPS) * g.astype(jnp.float32) + b.astype(jnp.float32)

def hybrid_layer(x, positions, w_in, b_gate, sinks, w_pa, w_pb, w_out, ln_g, ln_b):
    bn, s_len, _ = x.shape
    h = jnp.einsum('bsd,de->bse', x, w_in)
    (qa, ka, va, gate_a, qb, kb, vb, gate_b, mg_a, mg_b) = jnp.split(h, IN_OFFSETS, axis=-1)

    qa = apply_rope(qa.reshape(bn, s_len, A_HEADS, A_HEAD_DIM), positions)
    ka = apply_rope(ka.reshape(bn, s_len, A_KV_HEADS, A_HEAD_DIM), positions)
    va = va.reshape(bn, s_len, A_KV_HEADS, A_HEAD_DIM)
    qa = qa.reshape(bn, s_len, A_KV_HEADS, A_GROUP, A_HEAD_DIM)
    o_a, _ = banded_attention(pad_seq(qa), pad_seq(ka), pad_seq(va), A_WINDOW - 1,
                              sink=sinks.reshape(A_KV_HEADS, A_GROUP))
    o_a = o_a[:, :s_len].reshape(bn, s_len, A_WIDTH)

    n_b = B_N_GROUPS * B_HEADS_PER_GROUP
    qb = apply_rope(qb.reshape(bn, s_len, n_b, B_HEAD_DIM), positions)
    kb = apply_rope(kb.reshape(bn, s_len, n_b, B_HEAD_DIM), positions)
    vb = vb.reshape(bn, s_len, n_b, B_HEAD_DIM)
    outs, lses = [], []
    for gi, (window, dilation) in enumerate(B_PATTERNS):
        sl = slice(gi * B_HEADS_PER_GROUP, (gi + 1) * B_HEADS_PER_GROUP)
        o_g, lse_g = dilated_group(qb[:, :, sl], kb[:, :, sl], vb[:, :, sl], window, dilation)
        outs.append(o_g)
        lses.append(lse_g)
    wts = jax.nn.softmax(jnp.stack(lses, axis=0), axis=0)
    o_b = jnp.sum(wts[..., None] * jnp.stack(outs, axis=0), axis=0).reshape(bn, s_len, B_OUT_WIDTH)

    y_a = jnp.einsum('bse,ed->bsd', (o_a * jax.nn.silu(gate_a.astype(jnp.float32))).astype(x.dtype), w_pa)
    y_b = jnp.einsum('bse,ed->bsd', (o_b * jax.nn.silu(gate_b.astype(jnp.float32))).astype(x.dtype), w_pb)
    merged = jax.nn.sigmoid(mg_a + b_gate[0]) * y_a + jax.nn.sigmoid(mg_b + b_gate[1]) * y_b
    sub = jnp.einsum('bsd,de->bse', merged, w_out)

    out = layer_norm(DN_ALPHA * x.astype(jnp.float32) + sub.astype(jnp.float32), ln_g, ln_b)
    return out.astype(x.dtype)

def setup_inputs(seed: int = 0) -> dict:
    key = jax.random.key(seed)
    ks = jax.random.split(key, 10)
    x = jax.random.normal(ks[0], (BATCH, SEQ, D_MODEL), jnp.float32)
    positions = jnp.broadcast_to(jnp.arange(SEQ, dtype=jnp.int32)[None, :], (BATCH, SEQ))
    col_scale = np.concatenate([
        np.full((n,), DN_BETA if i in (2, 6) else 1.0, np.float32) for i, n in enumerate(IN_SIZES)])
    w_in = (jax.random.normal(ks[1], (DEPTH, D_MODEL, D_IN), jnp.float32)
            * (D_MODEL ** -0.5) * jnp.asarray(col_scale))
    b_gate = 0.01 * jax.random.normal(ks[2], (DEPTH, N_BRANCHES, D_MODEL), jnp.float32)
    sinks = 0.5 * jax.random.normal(ks[3], (DEPTH, A_HEADS), jnp.float32)
    w_pa = jax.random.normal(ks[4], (DEPTH, A_WIDTH, D_MODEL), jnp.float32) * (A_WIDTH ** -0.5) * DN_BETA
    w_pb = jax.random.normal(ks[5], (DEPTH, B_OUT_WIDTH, D_MODEL), jnp.float32) * (B_OUT_WIDTH ** -0.5) * DN_BETA
    w_out = jax.random.normal(ks[6], (DEPTH, D_MODEL, D_MODEL), jnp.float32) * (D_MODEL ** -0.5) * DN_BETA
    ln_g = 1.0 + 0.02 * jax.random.normal(ks[7], (DEPTH, D_MODEL), jnp.float32)
    ln_b = 0.02 * jax.random.normal(ks[8], (DEPTH, D_MODEL), jnp.float32)
    return {"x": x, "positions": positions, "w_in": w_in, "b_gate": b_gate, "sinks": sinks,
            "w_pa": w_pa, "w_pb": w_pb, "w_out": w_out, "ln_g": ln_g, "ln_b": ln_b}

def reference(x, positions, w_in, b_gate, sinks, w_pa, w_pb, w_out, ln_g, ln_b):
    for layer in range(DEPTH):
        x = hybrid_layer(x, positions, w_in[layer], b_gate[layer], sinks[layer], w_pa[layer],
                         w_pb[layer], w_out[layer], ln_g[layer], ln_b[layer])
    return x


_drawn_inputs = setup_inputs


def setup_inputs(seed=0):
    import zlib

    import numpy as np

    out = dict(_drawn_inputs(seed))
    spreads = {}
    factors = {'w_in': 3.684,
     'b_gate': 27.455,
     'sinks': 37.309,
     'w_pa': 5.534,
     'w_pb': 6.467,
     'w_out': 4.201,
     'ln_g': 7.989,
     'ln_b': 8.087}
    for name, (base, spread) in spreads.items():
        noise = np.random.default_rng([zlib.crc32(name.encode()), seed]).standard_normal(out[name].shape)
        drawn = base * np.exp(spread * noise) if base else spread * noise
        out[name] = __import__('jax').numpy.asarray(drawn.astype(out[name].dtype))
    for name, factor in factors.items():
        out[name] = (out[name] * factor).astype(out[name].dtype)
    return out
```

```python
from contextlib import ExitStack

import concourse.bass as bass
from concourse import mybir

F32 = mybir.dt.float32
F32R = mybir.dt.float32r
I32 = mybir.dt.int32
ALU = mybir.AluOpType
ACT = mybir.ActivationFunctionType

P = 128
SEQ = 512
D = 2048
NR = 4
KT = D // P
A_HEADS, A_KV, A_DH = 16, 2, 64
B_GROUPS, B_HEADS, B_DH = 3, 4, 128
A_WIDTH = A_HEADS * A_DH
KV_WIDTH = A_KV * A_DH
GW = B_HEADS * B_DH
QA = 0
KA = QA + A_WIDTH
GA = KA + 2 * KV_WIDTH
QB = GA + A_WIDTH
KB = QB + B_GROUPS * GW
VB = KB + B_GROUPS * GW
GB = VB + B_GROUPS * GW
MG = GB + GW
ALPHA = 2.0 ** 0.25
EPS = 1e-5
A_SCALE = A_DH ** -0.5
B_SCALE = B_DH ** -0.5
MASKED = -1.0e30

RING = 4
LOADS = 4
SLOT = 1024
PRO_JOBS = 12
A_ITERS, A_JOBS, A_UNITS = 4, 8, 8
B_JOBS, B_UNITS = 24, 4
M_ITERS, M_JOBS = 8, 12
O_ITERS, O_JOBS = 4, 8
AHEAD = 2


def job_a(i): return i * A_JOBS + PRO_JOBS
def job_b(h): return h * B_JOBS + (PRO_JOBS + A_ITERS * A_JOBS)
def job_m(n): return n * M_JOBS + (PRO_JOBS + A_ITERS * A_JOBS + B_HEADS * B_JOBS)
def job_o(n): return n * O_JOBS + (PRO_JOBS + A_ITERS * A_JOBS + B_HEADS * B_JOBS + M_ITERS * M_JOBS)


def fills_a(bank, i): return i + (1 if bank < 2 else 0)
def fills_b(bank, h): return h * (3 if bank < 3 else 2) + fills_a(bank, A_ITERS)
def fills_m(bank, n): return n * 2 + fills_b(bank, B_HEADS)
def fills_o(bank, n): return n + fills_m(bank, M_ITERS)


def unit_a(i): return i * A_UNITS
def unit_b(h): return h * B_UNITS + A_ITERS * A_UNITS


def stages(units, every, t, v, o):
    plan = {}
    for name, late in (("turn_out", o), ("values", v), ("turn_probs", t), ("scores", 0)):
        for u in range(units):
            plan.setdefault(u * every + late, []).append((name, u))
    return plan


A_PLAN = stages(A_UNITS, 3, 3, 5, 7)
B_PLAN = stages(B_UNITS, 6, 3, 5, 7)
B_PLAN_MERGE = stages(B_UNITS, 3, 2, 3, 4)


def groups(spec):
    job = 0
    for g, (jobs, banks) in enumerate(spec):
        for q in range(jobs):
            for bank in banks:
                yield job + q, g, q, bank, q == 0, q == jobs - 1
        job += jobs


A_BLOCKS = list(groups([(8, (0, 1, 2, 3))]))
B_BLOCKS = list(groups([(8, (0, 1, 2)), (8, (0, 1, 2, 3)), (8, (0, 1, 2, 3))]))
M_BLOCKS = list(groups([(4, (0, 1)), (4, (2, 3)), (2, (0, 1)), (2, (2, 3))]))
O_BLOCKS = list(groups([(8, (0, 1, 2, 3))]))


def build(nc, xT, x, pos, w_in, gate_bias, sinks, w_pa, w_pb, w_out, ln_g, ln_b, rope_rows, mask_a_in, mask_b_in, out):
    with ExitStack() as ctx:
        base = (nc.sbuf_base + 63) // 64 * 64
        fence = ctx.enter_context(nc.sbuf_tensor("arena", [P, (nc.sbuf_usable_end - base - 64) // 4], F32))
        del fence
        top = [base]

        def at(name, offset, shape, dt=F32):
            return nc.alloc_sbuf_tensor_at(name, shape, dt, offset=offset)

        def sb(name, shape, dt=F32):
            n = 4
            for s in shape[1:]:
                n *= s
            where, top[0] = top[0], top[0] + (n + 31) // 32 * 32
            assert top[0] <= nc.sbuf_usable_end
            return at(name, where, shape, dt)

        def sem(name):
            return ctx.enter_context(nc.semaphore(name))

        x_hi, x_lo = sb("x_hi", [P, KT, SEQ], F32R), sb("x_lo", [P, KT, SEQ], F32R)
        raw = sb("raw", [P, RING, SLOT])
        w_hi, w_lo = sb("w_hi", [P, RING, SLOT], F32R), sb("w_lo", [P, RING, SLOT], F32R)
        og_at = top[0]
        og_hi, og_lo = sb("og_hi", [P, 12, SEQ], F32R), sb("og_lo", [P, 12, SEQ], F32R)
        z = at("z", og_at, [P, NR, D])
        g_row, b_row = at("g_row", og_at + 4 * NR * D, [P, D]), at("b_row", og_at + 4 * (NR + 1) * D, [P, D])

        shared_at = top[0]
        q_b, k_b = sb("q_b", [P, B_GROUPS, SEQ]), sb("k_b", [P, B_GROUPS, SEQ])
        branch_at = top[0]
        v_b = sb("v_b", [P, NR, B_GROUPS * B_DH])
        mask_b = sb("mask_b", [P, NR * SEQ + 2 * P])
        probs_b = sb("probs_b", [P, SEQ + 2 * P])
        gate_b = sb("gate_b", [P, SEQ])
        q_a = at("q_a", branch_at, [P, 2, SEQ])
        gate_a = at("gate_a", branch_at + 4096, [P, 2, SEQ])
        k_a = at("k_a", branch_at + 8192, [P, A_KV, SEQ])
        v_a = at("v_a", branch_at + 12288, [P, 4, P])
        mask_a = at("mask_a", branch_at + 14336, [P, 2 * P])
        probs_a = at("probs_a", branch_at + 15360, [P, 2, 2, 2 * P + 3])
        angle, turns, rest = (at(n, shared_at + 2048 * k, [P, SEQ]) for k, n in enumerate(("angle", "turns", "rest")))
        pos_row = at("pos_row", shared_at + 3 * 2048, [P, SEQ], I32)
        k_rot = at("k_rot", shared_at + 4 * 2048, [P, SEQ])
        vT_a = at("vT_a", shared_at + 5 * 2048, [P, SEQ])
        merged = at("merged", shared_at, [P, KT, SEQ])

        probsT = sb("probsT", [P, 6, P])
        out_q = sb("out_q", [P, P])
        shifted = sb("shifted", [P, SEQ])
        tables_at = top[0]
        cos_a, sin_a, cos_b, sin_b = (sb(n, [P, SEQ]) for n in ("cos_a", "sin_a", "cos_b", "sin_b"))
        part_a, part_b = at("part_a", tables_at, [P, 2, SEQ]), at("part_b", tables_at + 4096, [P, 2, SEQ])
        ident = sb("ident", [P, P])
        rope_col = sb("rope_col", [P, 4])
        gbias = sb("gbias", [P, 2 * KT])
        sink_row = sb("sink_row", [P, A_HEADS])
        sink_pair = sb("sink_pair", [P, A_HEADS, 2])
        rowmax, negmax = sb("rowmax", [P, 2, 2]), sb("negmax", [P, 2, 2])
        denom, rdenom = sb("denom", [P, 2, 2]), sb("rdenom", [P, 2, 2])
        stats = sb("stats", [P, NR, O_ITERS, 6])
        variance, root, correction = sb("variance", [P, NR]), sb("root", [P, NR]), sb("correction", [P, NR])
        meanvar, rstd, shift = sb("meanvar", [P, NR, 2]), sb("rstd", [P, NR]), sb("shift", [P, NR])

        acc = [ctx.enter_context(nc.psum_tensor(f"acc{b}", [P, SEQ], F32)) for b in range(4)]
        ps_scores = ctx.enter_context(nc.psum_tensor("ps_scores", [P, 2 * SEQ], F32))
        ps_turn = ctx.enter_context(nc.psum_tensor("ps_turn", [P, SEQ], F32))
        ps_out = ctx.enter_context(nc.psum_tensor("ps_out", [P, SEQ], F32))

        raw_in = [sem(f"raw_in{s}") for s in range(RING)]
        hi_done, lo_done, slot_used = sem("hi_done"), sem("lo_done"), sem("slot_used")
        full, free = [sem(f"full{b}") for b in range(4)], [sem(f"free{b}") for b in range(4)]
        small_in, mask_b_in_sem, row_in, store = sem("small_in"), sem("mask_b_loaded"), sem("row_in"), sem("store")
        x_in = [sem(f"x_in{r}") for r in range(NR)]
        pos_in = sem("pos_in")
        ident_step, table_step, table_arg, table_done = sem("ident_step"), sem("table_step"), sem("table_arg"), sem("table_done")
        sink_step, sink_set = sem("sink_step"), sem("sink_set")
        rope_parts, rope_done = sem("rope_parts"), sem("rope_done")
        v_turned, v_a_ready = sem("v_turned"), sem("v_a_ready")
        sig_ready = sem("sig_ready")
        masked_ready = sem("masked_ready")
        scores_ready, rowmax_ready, negmax_ready = sem("scores_ready"), sem("rowmax_ready"), sem("negmax_ready")
        probs_ready, probsT_psum, probsT_ready = sem("probs_ready"), sem("probsT_psum"), sem("probsT_ready")
        probsT_tail, recip_ready, out_psum = sem("probsT_tail"), sem("recip_ready"), sem("out_psum")
        out_scaled, outT_psum, outT_used = sem("out_scaled"), sem("outT_psum"), sem("outT_used")
        og_hi_ready, og_ready = sem("og_hi_ready"), sem("og_ready")
        merge_sig, merged_ready = sem("merge_sig"), sem("merged_ready")
        merged_hi_ready, merged_lo_ready = sem("merged_hi_ready"), sem("merged_lo_ready")
        var_ready, root_ready = sem("var_ready"), sem("root_ready")
        stats_ready, ln_step, centred, scaled, finished = (sem("stats_ready"), sem("ln_step"), sem("centred"),
                                                           sem("scaled"), sem("finished"))

        w_in_v = w_in.rearrange("(k p) c -> p k c", p=P)
        w_pa_v = w_pa.rearrange("(k p) c -> p k c", p=P)
        w_pb_v = w_pb.rearrange("(k p) c -> p k c", p=P)
        w_out_v = w_out.rearrange("(k p) c -> p k c", p=P)
        xT_v = xT.rearrange("(k p) s -> p k s", p=P)
        x_v = x.rearrange("(j r) d -> r j d", r=NR)
        out_v = out.rearrange("b (j r) d -> r (b j) d", r=NR)

        def by_block(t):
            return t.rearrange("p (b r j) -> p r b j", b=4, r=NR)

        def by_residue(t):
            return t.rearrange("p (r b j) -> p r b j", b=4, r=NR)

        block = ctx.enter_context(nc.Block())

        @block.sync
        def _(sp):
            def job(n, first, off, pieces):
                slot = off % RING
                loads = reversed(list(pieces(raw[:, slot, :])))
                if not first:
                    sp.wait_ge(lo_done, n + (off - RING + 1))
                for dst, src in loads:
                    sp.dma_start(dst, src).then_inc(raw_in[slot], 16)

            def halves(dst, src):
                return [(dst[h:h + P // 2], src[h:h + P // 2]) for h in (0, P // 2)]

            def load_x(m):
                return lambda t: [part for k in range(2)
                                  for part in halves(t[:, SEQ * k:SEQ * k + SEQ], xT_v[:, 2 * m + k, :])]

            def load_kv(m):
                return lambda t: [(t[:, 256 * k:256 * k + 256], w_in_v[:, 4 * m + k, KA:GA]) for k in range(4)]

            def load_a(i, q):
                def pieces(t):
                    for half, col in enumerate((QA, GA)):
                        for k in range(2):
                            c = 512 * half + 256 * k
                            src = w_in_v[:, 2 * q + k, col:col + A_WIDTH].rearrange("p (v c) -> p v c", v=A_KV)
                            yield (t[:, c:c + 256].rearrange("p (v c) -> p v c", v=A_KV), src[:, :, bass.ds(i * P, P)])
                return pieces

            def load_b(h, g, q):
                def pieces(t):
                    col = (QB, KB, VB)[g]
                    for k in range(2):
                        c = (512 if g == 1 else 384) * k
                        src = w_in_v[:, 2 * q + k, col:col + B_GROUPS * GW].rearrange("p (g c) -> p g c", g=B_GROUPS)
                        dst = t[:, c:c + 384].rearrange("p (g c) -> p g c", g=B_GROUPS)
                        if g == 1:
                            yield dst, src[:, :, bass.ds(h * P, P)]
                            yield t[:, c + 384:c + 512], w_in_v[:, 2 * q + k, GB:GB + GW][:, bass.ds(h * P, P)]
                        else:
                            yield from halves(dst, src[:, :, bass.ds(h * P, P)])
                return pieces

            def load_m(n, g, q):
                def pieces(t):
                    cols = bass.ds(n * 256, 256)
                    for k in range(4):
                        if g < 2:
                            yield (t[:, 256 * k:256 * k + 256],
                                   w_in_v[:, 4 * q + k, MG + D * g:MG + D * (g + 1)][:, cols])
                        elif g == 2:
                            yield t[:, 256 * k:256 * k + 256], w_pa_v[:, 4 * q + k, cols]
                        elif k < 2:
                            yield from halves(t[:, 256 * k:256 * k + 256], w_pb_v[:, 2 * q + k, cols])
                return pieces

            def load_o(n, q):
                return lambda t: [part for k in range(2)
                                  for part in halves(t[:, 512 * k:512 * k + 512], w_out_v[:, 2 * q + k, bass.ds(n * 512, 512)])]

            n = 0
            for m in range(4):
                for piece in (load_x(2 * m), load_x(2 * m + 1), load_kv(m)):
                    job(0, n < RING, n, piece)
                    n += 1
                if m == 0:
                    sp.dma_start(rope_col[:], rope_rows).then_inc(pos_in, 16)
                    sp.dma_start(pos_row[:], pos.partition_broadcast(P)).then_inc(pos_in, 16)
            sp.dma_start(mask_a[:], mask_a_in).then_inc(small_in, 16)
            sp.dma_start(sink_row[:], sinks.partition_broadcast(P)).then_inc(small_in, 16)
            sp.dma_start(gbias[:], gate_bias).then_inc(small_in, 16)

            def iter_a(i):
                for q in range(A_JOBS):
                    job(job_a(i), False, q, load_a(i, q))

            def iter_b(h, first):
                for k in range(B_JOBS):
                    job(job_b(h), False, k, load_b(h, k // 8, k % 8))
                    if first and k == 15:
                        sp.wait_ge(og_ready, 2 * A_ITERS)
                        sp.dma_start(mask_b[:], mask_b_in).then_inc(mask_b_in_sem, 16)

            def iter_m(n):
                for k in range(M_JOBS):
                    g, q = ((0, k) if k < 4 else (1, k - 4) if k < 8 else (2, k - 8) if k < 10 else (3, k - 10))
                    job(job_m(n), False, k, load_m(n, g, q))

            def iter_o(n, first):
                for q in range(O_JOBS):
                    job(job_o(n), False, q, load_o(n, q))
                    if first and q == 3:
                        sp.wait_ge(full[3], fills_m(3, M_ITERS))
                        for r in range(NR):
                            sp.dma_start(z[:, r, :], x_v[r]).then_inc(x_in[r], 16)
                        sp.dma_start(g_row[:], ln_g.partition_broadcast(P)).then_inc(row_in, 16)
                        sp.dma_start(b_row[:], ln_b.partition_broadcast(P)).then_inc(row_in, 16)

            with sp.Fori(0, A_ITERS) as i:
                iter_a(i)
            iter_b(0, True)
            with sp.Fori(1, B_HEADS) as h:
                iter_b(h, False)
            with sp.Fori(0, M_ITERS) as n:
                iter_m(n)
            iter_o(0, True)
            with sp.Fori(1, O_ITERS) as n:
                iter_o(n, False)
            for r in range(NR):
                sp.wait_ge(finished, r + 1)
                sp.dma_start(out_v[r], z[:, r, :]).then_inc(store, 16)
            sp.wait_ge(store, 16 * NR)

        @block.gpsimd
        def _(pool):
            nc.gpsimd.memset(ident[:], 0.0).then_inc(ident_step, 1)
            pool.wait_ge(ident_step, 1)
            nc.gpsimd.affine_select(out=ident[:], in_=ident[:], compare_op=ALU.not_equal, fill=1.0, base=0,
                                    pattern=[[-1, P]], channel_multiplier=1).then_inc(ident_step, 1)

            def low(dst, slot, hi, n):
                pool.wait_ge(hi_done, n + 1)
                nc.gpsimd.tensor_tensor(dst, raw[:, slot, :], hi.bitcast(F32), ALU.subtract).then_inc(lo_done, 1)

            n = 0
            for m in range(4):
                for k in (2 * m, 2 * m + 1):
                    low(x_lo[:, 2 * k:2 * k + 2, :].rearrange("p k c -> p (k c)"), n % RING,
                        x_hi[:, 2 * k:2 * k + 2, :].rearrange("p k c -> p (k c)"), n)
                    n += 1
                low(w_lo[:, m, :], n % RING, w_hi[:, m, :], n)
                n += 1
            with pool.Fori(0, (job_o(O_ITERS) - PRO_JOBS) // RING) as i:
                for s in range(RING):
                    low(w_lo[:, s, :], s, w_hi[:, s, :], i * RING + (PRO_JOBS + s))
            pool.wait_ge(row_in, 32)
            for r in range(NR):
                pool.wait_ge(scaled, r + 1)
                nc.gpsimd.tensor_tensor(z[:, r, :], z[:, r, :], b_row[:], ALU.add).then_inc(finished, 1)

        @block.scalar
        def _(act):
            def high(n, off):
                s = off % RING
                act.wait_ge(raw_in[s], n * (16 * LOADS // RING) + 16 * LOADS * (off // RING + 1))
                act.wait_ge(slot_used, n + (off - 2 * RING - RING + 1))
                nc.scalar.activation(w_hi[:, s, :], raw[:, s, :], ACT.Copy).then_inc(hi_done, 1)

            def exps_a(u, a):
                b, j = divmod(u, 2)
                lo = P if b == 0 else 0
                act.wait_ge(negmax_ready, a + 1)
                for hh in range(2):
                    s = probs_a[:, j, hh, lo:2 * P + 1]
                    e = nc.scalar.activation(s, s, ACT.Exp, bias=negmax[:, j, hh:hh + 1], scale=A_SCALE,
                                             accum_out=denom[:, j, hh:hh + 1])
                e.then_inc(probs_ready, 1)

            def exps_b(u, a):
                act.wait_ge(negmax_ready, a + 1)
                nc.scalar.activation(probs_b[:], probs_b[:], ACT.Exp, bias=negmax[:, u % 2, 0:1], scale=B_SCALE,
                                     accum_out=denom[:, u % 2, 0:1]).then_inc(probs_ready, 1)

            def probs_out(kind, u, a):
                act.wait_ge(probsT_psum, a + 1)
                if kind == "b" or u:
                    act.wait_ge(out_psum, a)
                dst, src = probsT[:, 0:4, :], ps_turn.rearrange("p (c q) -> p c q", c=4)
                if kind == "a" and u < 2:
                    dst, src = (t.rearrange("p (v k) q -> p v k q", v=2)[:, :, 1, :] for t in (dst, src))
                nc.scalar.activation(dst, src, ACT.Copy).then_inc(probsT_ready, 1)

            def attend(kind, plan, g, first_unit):
                for stage, u in plan.get(g, ()):
                    if stage == "scores":
                        (exps_a if kind == "a" else exps_b)(u, first_unit + u)
                    if stage == "turn_probs":
                        probs_out(kind, u, first_unit + u)

            n = 0
            for m in range(4):
                for k in (2 * m, 2 * m + 1, None):
                    act.wait_ge(raw_in[n % RING], 16 * LOADS * (n // RING + 1))
                    dst = w_hi[:, m, :] if k is None else x_hi[:, 2 * k:2 * k + 2, :].rearrange("p k c -> p (k c)")
                    nc.scalar.activation(dst, raw[:, n % RING, :], ACT.Copy).then_inc(hi_done, 1)
                    n += 1
            for k, (table, col) in enumerate(((cos_b, None), (sin_b, 1), (cos_a, None), (sin_a, 3))):
                act.wait_ge(table_arg, k + 1)
                scale = 1.0 if col is None else rope_col[:, col:col + 1]
                nc.scalar.activation(table[:], rest[:], ACT.Sin, scale=scale).then_inc(table_done, 1)
            for off in range(AHEAD):
                high(job_a(0), off)
            act.wait_ge(full[1], 1)
            nc.scalar.activation(by_block(vT_a[:]), by_residue(acc[1][:]), ACT.Copy).then_inc(free[1], 1)

            def iter_a(i, with_attention):
                for g, (job, _, _, bank, _, last) in enumerate(A_BLOCKS):
                    if bank == 0:
                        high(job_a(i), job + AHEAD)
                    if with_attention:
                        attend("a", A_PLAN, g, unit_a(i - 1))
                    if not with_attention and g == 8:
                        act.wait_ge(v_turned, 1)
                        nc.scalar.activation(v_a[:], ps_turn.rearrange("p (b c) -> p b c", b=4), ACT.Copy)\
                            .then_inc(v_a_ready, 1)
                    if last and bank >= 2:
                        act.wait_ge(full[bank], fills_a(bank, i) + 1)
                        if with_attention and bank == 2:
                            act.wait_ge(og_ready, i * 2)
                        nc.scalar.activation(by_block(gate_a[:, bank - 2, :]), by_residue(acc[bank][:]), ACT.Sigmoid)\
                            .then_inc(sig_ready, 1)

            def iter_b(h, first):
                for g, (job, group, _, bank, _, last) in enumerate(B_BLOCKS):
                    if bank == 0:
                        high(job_b(h), job + AHEAD)
                    if first:
                        attend("a", A_PLAN, g, unit_a(A_ITERS - 1))
                    else:
                        attend("b", B_PLAN, g, unit_b(h - 1))
                    if last and group == 1 and bank == 3:
                        act.wait_ge(full[3], fills_b(3, h) + 1)
                        act.wait_ge(og_ready, h + 2 * A_ITERS)
                        nc.scalar.activation(gate_b[:], acc[3][:], ACT.Sigmoid).then_inc(sig_ready, 1)
                    if last and group == 2:
                        act.wait_ge(full[bank], fills_b(bank, h) + (3 if bank < 3 else 2))
                        act.wait_ge(out_psum, unit_b(h))
                        nc.scalar.activation(v_b[:, bank, :], acc[bank][:, 0:384], ACT.Copy).then_inc(free[bank], 1)

            def iter_m(n, first, last_iter):
                for g, (job, group, _, bank, _, last) in enumerate(M_BLOCKS):
                    if bank % 2 == 0:
                        high(job_m(n), job + AHEAD)
                    if first:
                        attend("b", B_PLAN_MERGE, g, unit_b(B_HEADS - 1))
                    if last and group < 2:
                        act.wait_ge(full[bank], fills_m(bank, n) + 1)
                        if not first and bank % 2 == 0:
                            act.wait_ge(merged_ready, n * 2)
                        part, t = (part_a, part_b)[group], bank % 2
                        nc.scalar.activation(part[:, t, :], acc[bank][:], ACT.Sigmoid,
                                             bias=gbias[:, bass.ds(n * 2 + (KT * group + t), 1)]).then_inc(merge_sig, 1)
                    if last_iter and group == 2 and job == 8 and bank == 1:
                        merged_high(0, 4, 12)
                        merged_high(4, 8, 12)
                    if last_iter and group == 2 and job == 9 and bank == 1:
                        merged_high(8, 12, 12)
                        merged_high(12, 14, 14)

            def merged_high(lo, hi, ready):
                act.wait_ge(merged_ready, ready)
                act.wait_ge(full[3], fills_m(3, M_ITERS - 1) + 1)
                nc.scalar.activation(x_hi[:, lo:hi, :], merged[:, lo:hi, :], ACT.Copy).then_inc(merged_hi_ready, 1)

            def iter_o(n, last_iter):
                for g, (job, _, _, bank, _, last) in enumerate(O_BLOCKS):
                    if bank == 0 and not (last_iter and job + AHEAD >= O_JOBS):
                        high(job_o(n), job + AHEAD)

            iter_a(0, False)
            with act.Fori(1, A_ITERS) as i:
                iter_a(i, True)
            iter_b(0, True)
            with act.Fori(1, B_HEADS) as h:
                iter_b(h, False)
            iter_m(0, True, False)
            with act.Fori(1, M_ITERS - 1) as n:
                iter_m(n, False, False)
            iter_m(M_ITERS - 1, False, True)
            merged_high(14, 16, 16)
            with act.Fori(0, O_ITERS - 1) as n:
                iter_o(n, False)
            iter_o(O_ITERS - 1, True)
            for r in range(NR):
                act.wait_ge(var_ready, r + 1)
                nc.scalar.activation(root[:, r:r + 1], variance[:, r:r + 1], ACT.Sqrt).then_inc(root_ready, 1)
                act.wait_ge(ln_step, 6 * r + 6)
                nc.scalar.activation(z[:, r, :], z[:, r, :], ACT.Identity, bias=shift[:, r:r + 1],
                                     scale=rstd[:, r:r + 1]).then_inc(centred, 1)

        @block.vector
        def _(dve):
            step = [0]

            def chain(instruction):
                step[0] += 1
                instruction.then_inc(table_step, 1)
                dve.wait_ge(table_step, step[0])

            two_pi = 6.283185307179586
            c1 = 6.28125
            c2 = 0.0019350051879882812
            c3 = two_pi - c1 - c2
            magic = 1.5 * 2.0 ** 23
            pi = 3.141592

            def reduce_angle(dst, src, unit, offset):
                chain(nc.vector.tensor_scalar(turns[:], src, 1.0 / (two_pi * unit), offset, ALU.mult, ALU.add))
                chain(nc.vector.tensor_scalar(turns[:], turns[:], magic, -magic, ALU.add, ALU.add))
                for k, c in enumerate((c1, c2, c3)):
                    chain(nc.vector.scalar_tensor_tensor(dst, turns[:], -c * unit, src if k == 0 else dst,
                                                         ALU.mult, ALU.add))

            dve.wait_ge(pos_in, 32)
            for k, (freq, quarter) in enumerate(((0, True), (0, False), (2, True), (2, False))):
                if quarter:
                    chain(nc.vector.tensor_copy(angle[:], pos_row[:]))
                    chain(nc.vector.tensor_scalar(angle[:], angle[:], rope_col[:, freq:freq + 1], None, ALU.mult))
                    reduce_angle(angle[:], angle[:], 65536.0, 0.0)
                if k:
                    dve.wait_ge(table_done, k)
                reduce_angle(rest[:], angle[:], 1.0, 0.25 if quarter else 0.0)
                chain(nc.vector.tensor_scalar(rest[:], rest[:], two_pi / 4 if quarter else 0.0, -pi, ALU.add, ALU.max))
                nc.vector.tensor_scalar(rest[:], rest[:], pi, None, ALU.min).then_inc(table_arg, 1)
            dve.wait_ge(small_in, 48)
            nc.vector.tensor_scalar(sink_pair[:, :, 0], sink_row[:], 1.0 / A_SCALE, None, ALU.mult).then_inc(sink_step, 1)
            nc.vector.tensor_scalar(sink_pair[:, :, 1], sink_row[:], -1.0, None, ALU.mult).then_inc(sink_step, 1)
            dve.wait_ge(sink_step, 2)
            dve.wait_ge(table_done, 4)

            def rope(dst, bank, filled, done, parts_done, half, cos, sin):
                dve.wait_ge(full[bank], filled)
                dve.wait_ge(rope_done, done)
                to_order, from_order = (by_block, by_residue) if half == 32 else (lambda t: t, lambda t: t)
                nc.vector.tensor_tensor(to_order(dst), from_order(acc[bank][:]), from_order(cos[:]), ALU.mult)\
                    .then_inc(rope_parts, 1)
                parts = P // half
                for k in range(parts):
                    to, frm = slice(half * k, half * (k + 1)), slice(half * (k ^ 1), half * ((k ^ 1) + 1))
                    last = nc.vector.tensor_tensor(to_order(shifted[to, :]), from_order(acc[bank][frm, :]),
                                                   from_order(sin[frm, :]), ALU.mult)
                    last.then_inc(free[bank] if k == parts - 1 else rope_parts, 1)
                dve.wait_ge(rope_parts, parts_done)
                dve.wait_ge(free[bank], filled)
                nc.vector.tensor_tensor(dst, dst, shifted[:], ALU.add).then_inc(rope_done, 1)

            parts_a, parts_b = 4, 2

            def mask_max_a(u, a):
                b, j = divmod(u, 2)
                lo = P if b == 0 else 0
                dve.wait_ge(scores_ready, a + 1)
                if u >= 2:
                    dve.wait_ge(probsT_psum, a - 1)
                nc.vector.tensor_copy(probs_a[:, j, :, 2 * P:2 * P + 1], probs_a[:, j, :, 2 * P + 1:2 * P + 2])
                masked = probs_a[:, j, :, lo:2 * P]
                nc.vector.tensor_tensor(masked, ps_scores[:].rearrange("p (h k) -> p h k", h=2)[:, :, lo:2 * P],
                                        mask_a[:, lo:2 * P].unsqueeze(1).to_broadcast([P, 2, 2 * P - lo]), ALU.add)\
                    .then_inc(masked_ready, 1)
                dve.wait_ge(masked_ready, a + 1)
                nc.vector.tensor_reduce(rowmax[:, j, :], masked, mybir.AxisListType.X, ALU.max).then_inc(rowmax_ready, 1)
                dve.wait_ge(rowmax_ready, a + 1)
                nc.vector.scalar_tensor_tensor(negmax[:, j, :], rowmax[:, j, :], -A_SCALE, probs_a[:, j, :, 2 * P + 2],
                                               ALU.mult, ALU.min).then_inc(negmax_ready, 1)

            def mask_max_b(u, a):
                dve.wait_ge(scores_ready, a + 1)
                dve.wait_ge(probsT_psum, a)
                nc.vector.tensor_tensor(probs_b[:, 0:SEQ], ps_scores[:, 0:SEQ], mask_b[:, u * SEQ:(u + 1) * SEQ], ALU.add)
                nc.vector.tensor_tensor(probs_b[:, SEQ:SEQ + 2 * P], ps_scores[:, SEQ:SEQ + 2 * P],
                                        mask_b[:, NR * SEQ:NR * SEQ + 2 * P], ALU.add).then_inc(masked_ready, 1)
                dve.wait_ge(masked_ready, a + 1)
                nc.vector.tensor_reduce(rowmax[:, u % 2, 0:1], probs_b[:], mybir.AxisListType.X, ALU.max)\
                    .then_inc(rowmax_ready, 1)
                dve.wait_ge(rowmax_ready, a + 1)
                nc.vector.tensor_scalar(negmax[:, u % 2, 0:1], rowmax[:, u % 2, 0:1], -B_SCALE, None, ALU.mult)\
                    .then_inc(negmax_ready, 1)

            def probs_tail(u, a, h):
                dve.wait_ge(probsT_psum, a + 1)
                dve.wait_ge(out_psum, a)
                nc.vector.tensor_copy(probsT[:, 4:6, :], ps_scores[:, SEQ + 2 * P:2 * SEQ].rearrange("p (c q) -> p c q", c=2))\
                    .then_inc(probsT_tail, 1)

            def scale_out(kind, u, a):
                j = u % 2
                dve.wait_ge(probs_ready, a + 1)
                n = 2 if kind == "a" else 1
                nc.vector.reciprocal(rdenom[:, j, 0:n], denom[:, j, 0:n]).then_inc(recip_ready, 1)
                dve.wait_ge(out_psum, a + 1)
                dve.wait_ge(recip_ready, a + 1)
                if kind == "a":
                    shape = [P, 2, A_DH]
                    nc.vector.tensor_tensor(out_q[:].rearrange("p (h d) -> p h d", h=2),
                                            ps_out[:, 0:P].rearrange("p (h d) -> p h d", h=2),
                                            rdenom[:, j, :].unsqueeze(2).to_broadcast(shape), ALU.mult)\
                        .then_inc(out_scaled, 1)
                else:
                    nc.vector.tensor_scalar(out_q[:], ps_out[:, 0:P], rdenom[:, j, 0:1], None, ALU.mult)\
                        .then_inc(out_scaled, 1)

            def split_gated(kind, gated, tile, done):
                hi, lo = (t[:, bass.ds(tile, 1), :].rearrange("p t s -> p (t s)") for t in (og_hi, og_lo))
                if kind == "a":
                    hi, lo, gated = by_residue(hi), by_residue(lo), by_block(gated)
                nc.vector.tensor_copy(hi, gated).then_inc(og_hi_ready, 1)
                dve.wait_ge(og_hi_ready, done + 1)
                nc.vector.tensor_tensor(lo, gated, hi.bitcast(F32), ALU.subtract).then_inc(og_ready, 1)

            def gate_out(kind, u, a, i):
                dve.wait_ge(outT_psum, a + 1)
                b, j = divmod(u, 2)
                g = gate_a[:, j, b * P:(b + 1) * P] if kind == "a" else gate_b[:, u * P:(u + 1) * P]
                nc.vector.tensor_tensor(g, ps_out[:, P:2 * P], g, ALU.mult).then_inc(outT_used, 1)
                if kind == "a" and b == 3:
                    dve.wait_ge(outT_used, a + 1)
                    split_gated(kind, gate_a[:, j, :], i + A_ITERS * j, i * 2 + j)
                if kind == "b" and u == 3:
                    dve.wait_ge(outT_used, a + 1)
                    split_gated(kind, gate_b[:], i + 2 * A_ITERS, i + 2 * A_ITERS)

            def attend(kind, plan, g, first_unit, i):
                if kind == "a" and g == 0:
                    nc.vector.tensor_copy(probs_a[:, :, :, 2 * P + 1:2 * P + 3].rearrange("p j v c -> p (j v) c"),
                                          sink_pair[:, bass.ds(i * 4, 4), :]).then_inc(sink_set, 1)
                    dve.wait_ge(sink_set, i + 1)
                if kind == "b" and g == 0:
                    dve.wait_ge(mask_b_in_sem, 16)
                for stage, u in plan.get(g, ()):
                    a = first_unit + u
                    if stage == "scores":
                        (mask_max_a if kind == "a" else mask_max_b)(u, a)
                    elif stage == "turn_probs" and kind == "b":
                        probs_tail(u, a, i)
                    elif stage == "values":
                        scale_out(kind, u, a)
                    elif stage == "turn_out":
                        gate_out(kind, u, a, i)

            def gate(dst, src, bank, done):
                dve.wait_ge(sig_ready, done + 1)
                nc.vector.tensor_tensor(dst, src, dst, ALU.mult).then_inc(free[bank], 1)

            rope(k_rot[:], 0, 1, 0, parts_a, 32, cos_a, sin_a)
            dve.wait_ge(rope_done, 1)
            for kv in range(A_KV):
                for hh in range(2):
                    nc.vector.tensor_copy(k_a[A_DH * hh:A_DH * hh + A_DH, kv, :], k_rot[A_DH * kv:A_DH * kv + A_DH, :])\
                        .then_inc(rope_done, 1)

            def iter_a(i, with_attention):
                for g, (job, _, _, bank, _, last) in enumerate(A_BLOCKS):
                    if with_attention:
                        attend("a", A_PLAN, g, unit_a(i - 1), i - 1)
                    if last and bank < 2:
                        if with_attention and bank == 0:
                            dve.wait_ge(scores_ready, unit_a(i))
                        rope(q_a[:, bank, :], bank, fills_a(bank, i) + 1, i * 2 + (5 + bank),
                             i * (2 * parts_a) + parts_a * (bank + 2), 32, cos_a, sin_a)
                    elif last:
                        gate(by_block(gate_a[:, bank - 2, :]), by_residue(acc[bank][:]), bank, i * 2 + (bank - 2))

            all_a = parts_a * (1 + 2 * A_ITERS)

            def iter_b(h, first):
                for g, (job, group, _, bank, _, last) in enumerate(B_BLOCKS):
                    if first:
                        attend("a", A_PLAN, g, unit_a(A_ITERS - 1), A_ITERS - 1)
                    else:
                        attend("b", B_PLAN, g, unit_b(h - 1), h - 1)
                    if last and group < 2 and bank < 3:
                        if not first and group == 0 and bank == 0:
                            dve.wait_ge(scores_ready, unit_b(h))
                        tile = h * (6 * parts_b) + (all_a + parts_b * (3 * group + bank + 1))
                        rope((q_b, k_b)[group][:, bank, :], bank, fills_b(bank, h) + (group + 1),
                             h * 6 + (5 + 2 * A_ITERS + 3 * group + bank), tile, 64, cos_b, sin_b)
                    if last and group == 1 and bank == 3:
                        gate(gate_b[:], acc[3][:], 3, h + 2 * A_ITERS)

            def iter_m(n, first):
                for g, (job, group, _, bank, _, last) in enumerate(M_BLOCKS):
                    if first:
                        attend("b", B_PLAN_MERGE, g, unit_b(B_HEADS - 1), B_HEADS - 1)
                    if last and group < 2:
                        dve.wait_ge(merge_sig, n * 4 + (2 * group + bank % 2 + 1))
                        dve.sem_inc(free[bank], 1)
                    if last and group >= 2:
                        t = bank % 2
                        part = (part_a, part_b)[group - 2]
                        dve.wait_ge(full[bank], fills_m(bank, n) + 2)
                        nc.vector.tensor_tensor(part[:, t, :], acc[bank][:], part[:, t, :], ALU.mult)\
                            .then_inc(free[bank], 1)
                        if group == 3:
                            dve.wait_ge(free[bank], fills_m(bank, n) + 2)
                            dve.wait_ge(free[t], fills_m(t, n) + 2)
                            nc.vector.tensor_tensor(merged[:, bass.ds(n * 2 + t, 1), :].rearrange("p k c -> p (k c)"),
                                                    part_a[:, t, :], part_b[:, t, :], ALU.add).then_inc(merged_ready, 1)
                    if isinstance(n, int) and n == M_ITERS - 1 and group == 3 and job == 10 and bank == 3:
                        for c in range(3):
                            merged_low(4 * c, 4 * c + 4, c + 1)
                        merged_low(12, 14, 4)

            def merged_low(lo, hi, ready):
                dve.wait_ge(merged_hi_ready, ready)
                nc.vector.tensor_tensor(x_lo[:, lo:hi, :], merged[:, lo:hi, :], x_hi[:, lo:hi, :].bitcast(F32),
                                        ALU.subtract).then_inc(merged_lo_ready, 1)

            def iter_o(n, last_iter):
                for r in range(NR):
                    dve.wait_ge(full[r], fills_o(r, n) + 1)
                    if isinstance(n, int) and n == 0:
                        dve.wait_ge(x_in[r], 16)
                    chunk = z[:, r, bass.ds(n * SEQ, SEQ)]
                    nc.vector.scalar_tensor_tensor(chunk, chunk, ALPHA, acc[r][:], ALU.mult, ALU.add)\
                        .then_inc(free[r], 1)
                    dve.wait_ge(free[r], fills_o(r, n) + 1)
                    nc.vector.bn_stats(stats[:, r, bass.ds(n, 1), :].rearrange("p n s -> p (n s)"), chunk)\
                        .then_inc(stats_ready, 1)
                    if not last_iter:
                        continue
                    dve.wait_ge(stats_ready, NR * n + r + 1)
                    nc.vector.bn_aggr(meanvar[:, r, :], stats[:, r, :, :].rearrange("p n s -> p (n s)"))\
                        .then_inc(ln_step, 1)
                    dve.wait_ge(ln_step, 6 * r + 1)
                    var, inv, cor = variance[:, r:r + 1], rstd[:, r:r + 1], correction[:, r:r + 1]
                    nc.vector.tensor_scalar(var, meanvar[:, r, 1:2], EPS, None, ALU.add).then_inc(var_ready, 1)
                    dve.wait_ge(root_ready, r + 1)
                    nc.vector.reciprocal(inv, root[:, r:r + 1]).then_inc(ln_step, 1)
                    dve.wait_ge(ln_step, 6 * r + 2)
                    nc.vector.tensor_scalar(cor, inv, inv, var, ALU.mult, ALU.mult).then_inc(ln_step, 1)
                    dve.wait_ge(ln_step, 6 * r + 3)
                    nc.vector.tensor_scalar(cor, cor, -0.5, 1.5, ALU.mult, ALU.add).then_inc(ln_step, 1)
                    dve.wait_ge(ln_step, 6 * r + 4)
                    nc.vector.tensor_scalar(inv, inv, cor, None, ALU.mult).then_inc(ln_step, 1)
                    dve.wait_ge(ln_step, 6 * r + 5)
                    nc.vector.tensor_scalar(shift[:, r:r + 1], meanvar[:, r, 0:1], inv, -1.0,
                                            ALU.mult, ALU.mult).then_inc(ln_step, 1)
                    if r:
                        gain(r - 1)
                if last_iter:
                    gain(NR - 1)

            def gain(r):
                if r == 0:
                    dve.wait_ge(row_in, 32)
                dve.wait_ge(centred, r + 1)
                nc.vector.tensor_tensor(z[:, r, :], z[:, r, :], g_row[:], ALU.mult).then_inc(scaled, 1)

            iter_a(0, False)
            with dve.Fori(1, A_ITERS) as i:
                iter_a(i, True)
            iter_b(0, True)
            with dve.Fori(1, B_HEADS) as h:
                iter_b(h, False)
            iter_m(0, True)
            with dve.Fori(1, M_ITERS - 1) as n:
                iter_m(n, False)
            iter_m(M_ITERS - 1, False)
            merged_low(14, 16, 5)
            iter_o(0, False)
            with dve.Fori(1, O_ITERS - 1) as n:
                iter_o(n, False)
            iter_o(O_ITERS - 1, True)

        @block.tensor
        def _(pe):
            started = [False]

            def products(bank, pairs, cols, start, stop, new_job):
                n = 3 * len(pairs)
                k = 0
                for s_hi, s_lo, m_hi, m_lo in pairs:
                    for s, m in ((s_hi, m_hi), (s_hi, m_lo), (s_lo, m_hi)):
                        ins = nc.tensor.matmul(acc[bank][:, 0:cols], s, m, start=start and k == 0, stop=stop and k == n - 1)
                        if k == 0 and new_job and started[0]:
                            ins.then_inc(slot_used, 1)
                        started[0] = True
                        k += 1
                if stop:
                    ins.then_inc(full[bank], 1)

            def x_moving(k):
                return x_hi[:, k, :], x_lo[:, k, :]

            def scores_a(u):
                b, j = divmod(u, 2)
                for hh in range(2):
                    rows, c = slice(A_DH * hh, A_DH * hh + A_DH), hh * SEQ
                    lo = P if b == 0 else 0
                    last = nc.tensor.matmul(ps_scores[:, c + lo:c + 2 * P], q_a[rows, j, b * P:b * P + P],
                                            k_a[rows, j, (b - 1) * P + lo:(b + 1) * P], start=True, stop=True)
                last.then_inc(scores_ready, 1)

            def scores_b(u):
                q = slice(u * P, u * P + P)
                nc.tensor.matmul(ps_scores[:, 0:SEQ], q_b[:, 0, q], k_b[:, 0, :], start=True, stop=True)
                nc.tensor.matmul(ps_scores[:, SEQ:SEQ + P], q_b[:, 1, q], k_b[:, 1, q], start=True, stop=True)
                nc.tensor.matmul(ps_scores[:, SEQ + P:SEQ + 2 * P], q_b[:, 2, q], k_b[:, 2, q], start=True, stop=True)\
                    .then_inc(scores_ready, 1)

            def attend(kind, plan, g, first_unit, i):
                for stage, u in plan.get(g, ()):
                    a = first_unit + u
                    if stage == "scores":
                        if kind == "a":
                            if u == 0:
                                pe.wait_ge(rope_done, i * 2 + 7)
                            if u:
                                pe.wait_ge(negmax_ready, a)
                            scores_a(u)
                        else:
                            if u == 0:
                                pe.wait_ge(rope_done, i * 6 + (2 * A_ITERS + 5 + 6))
                            pe.wait_ge(negmax_ready, a)
                            if not u == 0:
                                pe.wait_ge(probsT_tail, a - unit_b(0))
                            scores_b(u)
                    elif stage == "turn_probs":
                        pe.wait_ge(probs_ready, a + 1)
                        if kind == "b" or u:
                            pe.wait_ge(probsT_ready, a)
                        if kind == "a":
                            b, j = divmod(u, 2)
                            for hh in range(2):
                                for kb in ((1,) if b == 0 else (0, 1)):
                                    c = (2 * hh + kb) * P
                                    last = nc.tensor.transpose(ps_turn[:, c:c + P], probs_a[:, j, hh, kb * P:kb * P + P],
                                                               ident[:])
                        else:
                            for c in range(6):
                                dst = ps_turn[:, c * P:c * P + P] if c < 4 else ps_scores[:, (c + 2) * P:(c + 3) * P]
                                last = nc.tensor.transpose(dst, probs_b[:, c * P:c * P + P], ident[:])
                        last.then_inc(probsT_psum, 1)
                    elif stage == "values":
                        pe.wait_ge(probsT_ready, a + 1)
                        if kind == "b" or u:
                            pe.wait_ge(outT_used, a)
                        if kind == "a":
                            b, j = divmod(u, 2)
                            kbs = (1,) if b == 0 else (0, 1)
                            for hh in range(2):
                                for kb in kbs:
                                    last = nc.tensor.matmul(ps_out[:, A_DH * hh:A_DH * hh + A_DH], probsT[:, 2 * hh + kb, :],
                                                            v_a[:, b - 1 + kb, A_DH * j:A_DH * j + A_DH],
                                                            start=kb == kbs[0], stop=kb == 1)
                        else:
                            pe.wait_ge(probsT_tail, a - unit_b(0) + 1)
                            if u == 0:
                                for bank in range(4):
                                    pe.wait_ge(free[bank], fills_b(bank, i + 1))
                            for c in range(6):
                                tile, grp = (c, 0) if c < 4 else (u, c - 3)
                                last = nc.tensor.matmul(ps_out[:, 0:P], probsT[:, c, :], v_b[:, tile, grp * P:grp * P + P],
                                                        start=c == 0, stop=c == 5)
                        last.then_inc(out_psum, 1)
                    else:
                        pe.wait_ge(out_scaled, a + 1)
                        nc.tensor.transpose(ps_out[:, P:2 * P], out_q[:], ident[:]).then_inc(outT_psum, 1)

            for m in range(4):
                pe.wait_ge(lo_done, 3 * m + 3)
                for bank in range(2):
                    pairs = []
                    for k in range(4):
                        c = slice(256 * k + P * bank, 256 * k + P * bank + P)
                        pairs.append((w_hi[:, m, c], w_lo[:, m, c], *x_moving(4 * m + k)))
                    products(bank, pairs, SEQ, m == 0, m == 3, bank == 0)

            def ready(n, off):
                pe.wait_ge(lo_done, n + (off + 1))

            def iter_a(i, with_attention):
                for g, (job, _, q, bank, first, last) in enumerate(A_BLOCKS):
                    if with_attention:
                        attend("a", A_PLAN, g, unit_a(i - 1), i - 1)
                    elif g == 8:
                        pe.wait_ge(free[1], 1)
                        pe.wait_ge(ident_step, 2)
                        for b in range(4):
                            t = nc.tensor.transpose(ps_turn[:, b * P:b * P + P], vT_a[:, b * P:b * P + P], ident[:])
                        t.then_inc(v_turned, 1)
                    if bank == 0:
                        ready(job_a(i), job)
                    if first and not (not with_attention and bank >= 2):
                        pe.wait_ge(free[bank], fills_a(bank, i))
                    s, (half, j) = job % RING, divmod(bank, 2)
                    pairs = []
                    for k in range(2):
                        c = 512 * half + 256 * k + P * j
                        pairs.append((w_hi[:, s, c:c + P], w_lo[:, s, c:c + P], *x_moving(2 * q + k)))
                    products(bank, pairs, SEQ, first, last, bank == 0)

            def iter_b(h, first_iter):
                for g, (job, group, q, bank, first, last) in enumerate(B_BLOCKS):
                    if first_iter:
                        attend("a", A_PLAN, g, unit_a(A_ITERS - 1), A_ITERS - 1)
                    else:
                        attend("b", B_PLAN, g, unit_b(h - 1), h - 1)
                    if bank == 0:
                        ready(job_b(h), job)
                    if first:
                        pe.wait_ge(free[bank], fills_b(bank, h) + (group - (1 if bank == 3 else 0)))
                    s = job % RING
                    pairs = []
                    for k in range(2):
                        if group == 2:
                            c, r = slice(384 * k, 384 * k + 384), slice(bank * P, bank * P + P)
                            kk = 2 * q + k
                            pairs.append((x_hi[:, kk, r], x_lo[:, kk, r], w_hi[:, s, c], w_lo[:, s, c]))
                        else:
                            c = (384, 512)[group] * k + bank * P
                            pairs.append((w_hi[:, s, c:c + P], w_lo[:, s, c:c + P], *x_moving(2 * q + k)))
                    products(bank, pairs, 384 if group == 2 else SEQ, first, last, bank == 0)

            def iter_m(n, first_iter):
                for g, (job, group, q, bank, first, last) in enumerate(M_BLOCKS):
                    if first_iter:
                        attend("b", B_PLAN_MERGE, g, unit_b(B_HEADS - 1), B_HEADS - 1)
                    if bank % 2 == 0:
                        ready(job_m(n), job)
                    if first:
                        pe.wait_ge(free[bank], fills_m(bank, n) + group // 2)
                        if first_iter and bank % 2 == 0 and group >= 2:
                            pe.wait_ge(og_ready, (8, 12)[group - 2])
                    s, t = job % RING, bank % 2
                    pairs = []
                    for k in range(4 if group < 3 else 2):
                        c = slice(256 * k + P * t, 256 * k + P * t + P)
                        if group < 2:
                            moving = x_moving(4 * q + k)
                        else:
                            e = 4 * q + k if group == 2 else 8 + 2 * q + k
                            moving = og_hi[:, e, :], og_lo[:, e, :]
                        pairs.append((w_hi[:, s, c], w_lo[:, s, c], *moving))
                    products(bank, pairs, SEQ, first, last, bank % 2 == 0)

            def iter_o(n, first_iter):
                for job, _, q, bank, first, last in O_BLOCKS:
                    if bank == 0:
                        ready(job_o(n), job)
                        if first_iter:
                            pe.wait_ge(merged_lo_ready, (1, 1, 2, 2, 3, 3, 4, 5)[q])
                    if first:
                        pe.wait_ge(free[bank], fills_o(bank, n))
                    s, r = job % RING, slice(bank * P, bank * P + P)
                    pairs = [(x_hi[:, 2 * q + k, r], x_lo[:, 2 * q + k, r], w_hi[:, s, 512 * k:512 * k + 512],
                              w_lo[:, s, 512 * k:512 * k + 512]) for k in range(2)]
                    products(bank, pairs, SEQ, first, last, bank == 0)

            iter_a(0, False)
            pe.wait_ge(v_a_ready, 1)
            with pe.Fori(1, A_ITERS) as i:
                iter_a(i, True)
            iter_b(0, True)
            with pe.Fori(1, B_HEADS) as h:
                iter_b(h, False)
            iter_m(0, True)
            with pe.Fori(1, M_ITERS) as n:
                iter_m(n, False)
            iter_o(0, True)
            with pe.Fori(1, O_ITERS) as n:
                iter_o(n, False)


def kernel(x, positions, w_in, b_gate, sinks, w_pa, w_pb, w_out, ln_g, ln_b):
    import numpy as np
    import concourse.bacc as bacc
    from concourse.bass_utils import run_bass_kernel_spmd

    x, positions, w_in, b_gate, sinks, w_pa, w_pb, w_out, ln_g, ln_b = (
        np.asarray(a) for a in (x, positions, w_in, b_gate, sinks, w_pa, w_pb, w_out, ln_g, ln_b))
    t = (4 * np.arange(P)[None, :] + np.arange(NR)[:, None]).reshape(-1)

    p = np.arange(P)
    rope_rows = np.stack([10000.0 ** (-(p % 64) / 64.0), np.where(p < 64, 1.0, -1.0),
                          10000.0 ** (-(p % 32) / 32.0), np.where(p % 64 < 32, 1.0, -1.0)], axis=1).astype(np.float32)
    in_block = (4 * np.arange(32)[None, :] + np.arange(NR)[:, None]).reshape(-1)
    dist = in_block[:, None] - np.concatenate([in_block - P, in_block])[None, :]
    mask_a = np.where((dist >= 0) & (dist < 128), 0.0, MASKED).astype(np.float32)
    far = t.reshape(NR, P)[:, :, None] - t[None, None, :]
    near = np.where((far >= 0) & (far <= 128), 0.0, MASKED).transpose(1, 0, 2).reshape(P, NR * SEQ)
    step = p[:, None] - p[None, :]
    by4 = np.where(step >= 0, 0.0, MASKED)
    by16 = np.where((step >= 0) & (step % 4 == 0), 0.0, MASKED)
    mask_b = np.concatenate([near, by4, by16], axis=1).astype(np.float32)

    arrays = {
        "xT": np.ascontiguousarray(x[0].T[:, t]),
        "x": x[0],
        "pos": np.ascontiguousarray(positions[0][t]),
        "w_in": w_in[0],
        "gate_bias": np.ascontiguousarray(b_gate[0].reshape(2 * KT, P).T),
        "sinks": np.ascontiguousarray(sinks[0].reshape(A_KV, A_ITERS, 2).transpose(1, 0, 2).reshape(A_HEADS)),
        "w_pa": w_pa[0], "w_pb": w_pb[0], "w_out": w_out[0], "ln_g": ln_g[0], "ln_b": ln_b[0],
        "rope_rows": rope_rows, "mask_a": mask_a, "mask_b": mask_b,
    }
    nc = bacc.Bacc("TRN2", target_bir_lowering=False, num_devices=1)
    args = [nc.dram_tensor(n, a.shape, mybir.dt.from_np(a.dtype), kind="ExternalInput").ap() for n, a in arrays.items()]
    out = nc.dram_tensor("out", (1, SEQ, D), F32, kind="ExternalOutput").ap()
    build(nc, *args, out)
    run = run_bass_kernel_spmd(nc, [arrays], core_ids=[0])
    return run.results[0]["out"]
```

```python
from contextlib import ExitStack

import concourse.bass as bass
from concourse import mybir

F32 = mybir.dt.float32
F32R = mybir.dt.float32r
I32 = mybir.dt.int32
ALU = mybir.AluOpType
ACT = mybir.ActivationFunctionType

P = 128
SEQ = 512
D = 2048
NR = 4
KT = D // P
A_HEADS, A_KV, A_DH = 16, 2, 64
B_GROUPS, B_HEADS, B_DH = 3, 4, 128
A_WIDTH = A_HEADS * A_DH
KV_WIDTH = A_KV * A_DH
GW = B_HEADS * B_DH
QA = 0
KA = QA + A_WIDTH
GA = KA + 2 * KV_WIDTH
QB = GA + A_WIDTH
KB = QB + B_GROUPS * GW
VB = KB + B_GROUPS * GW
GB = VB + B_GROUPS * GW
MG = GB + GW
ALPHA = 2.0 ** 0.25
EPS = 1e-5
A_SCALE = A_DH ** -0.5
B_SCALE = B_DH ** -0.5
MASKED = -1.0e30

RING = 4
LOADS = 4
SLOT = 1024
PRO_JOBS = 12
A_ITERS, A_JOBS, A_UNITS = 4, 8, 8
B_JOBS, B_UNITS = 24, 4
M_ITERS, M_JOBS = 8, 12
O_ITERS, O_JOBS = 4, 8
AHEAD = 2


def job_a(i): return i * A_JOBS + PRO_JOBS
def job_b(h): return h * B_JOBS + (PRO_JOBS + A_ITERS * A_JOBS)
def job_m(n): return n * M_JOBS + (PRO_JOBS + A_ITERS * A_JOBS + B_HEADS * B_JOBS)
def job_o(n): return n * O_JOBS + (PRO_JOBS + A_ITERS * A_JOBS + B_HEADS * B_JOBS + M_ITERS * M_JOBS)


def fills_a(bank, i): return i
def fills_b(bank, h): return h * (3 if bank < 3 else 2) + fills_a(bank, A_ITERS)
def fills_m(bank, n): return n * 2 + fills_b(bank, B_HEADS)
def fills_o(bank, n): return n + fills_m(bank, M_ITERS)


def unit_a(i): return i * A_UNITS
def unit_b(h): return h * B_UNITS + A_ITERS * A_UNITS


def stages(units, start, every, t, v, o):
    plan = {}
    for name, late in (("turn_out", o), ("values", v), ("turn_probs", t), ("scores", 0)):
        for u in range(units):
            plan.setdefault(start + u * every + late, []).append((name, u))
    return plan


A_PLAN = stages(A_UNITS, 1, 3, 3, 5, 6)
B_PLAN = stages(B_UNITS, 1, 6, 3, 5, 7)
B_PLAN_MERGE = stages(B_UNITS, 0, 3, 2, 3, 4)


def groups(spec, together=2):
    job = 0
    for g, (jobs, banks) in enumerate(spec):
        apart = jobs - together
        order = [(q, bank) for q in range(apart) for bank in banks]
        order += [(q, bank) for bank in banks for q in range(apart, jobs)]
        for n, (q, bank) in enumerate(order):
            released = n == 0 or order[n - 1][1] == banks[-1]
            yield job + q, g, q, bank, q == 0, q == jobs - 1, bank == banks[0], released
        job += jobs


A_BLOCKS = list(groups([(8, (0, 1, 2, 3))]))
B_BLOCKS = list(groups([(8, (0, 1, 2)), (8, (0, 1, 2, 3)), (8, (0, 1, 2, 3))]))
M_BLOCKS = list(groups([(4, (0, 1)), (4, (2, 3)), (2, (0, 1)), (2, (2, 3))], 1))
O_BLOCKS = list(groups([(8, (0, 1, 2, 3))], 1))
O_BLOCKS_LAST = list(groups([(8, (0, 1, 2, 3))], RING))
LN_SPLIT = 1408


def build(nc, xT, x, pos, w_in, gate_bias, sinks, w_pa, w_pb, w_out, ln_g, ln_b, rope_rows, mask_a_in, mask_b_in, out):
    with ExitStack() as ctx:
        base = (nc.sbuf_base + 63) // 64 * 64
        fence = ctx.enter_context(nc.sbuf_tensor("arena", [P, (nc.sbuf_usable_end - base - 64) // 4], F32))
        del fence
        top = [base]

        def at(name, offset, shape, dt=F32):
            return nc.alloc_sbuf_tensor_at(name, shape, dt, offset=offset)

        def sb(name, shape, dt=F32):
            n = 4
            for s in shape[1:]:
                n *= s
            where, top[0] = top[0], top[0] + (n + 31) // 32 * 32
            assert top[0] <= nc.sbuf_usable_end
            return at(name, where, shape, dt)

        def sem(name):
            return ctx.enter_context(nc.semaphore(name))

        x_hi, x_lo = sb("x_hi", [P, KT, SEQ], F32R), sb("x_lo", [P, KT, SEQ], F32R)
        raw = sb("raw", [P, RING, SLOT])
        w_hi, w_lo = sb("w_hi", [P, RING, SLOT], F32R), sb("w_lo", [P, RING, SLOT], F32R)
        og_at = top[0]
        og_hi, og_lo = sb("og_hi", [P, 12, SEQ], F32R), sb("og_lo", [P, 12, SEQ], F32R)
        z = at("z", og_at, [P, NR, D])
        g_row, b_row = at("g_row", og_at + 4 * NR * D, [P, D]), at("b_row", og_at + 4 * (NR + 1) * D, [P, D])

        shared_at = top[0]
        q_b, k_b = sb("q_b", [P, B_GROUPS, SEQ]), sb("k_b", [P, B_GROUPS, SEQ])
        branch_at = top[0]
        v_b = sb("v_b", [P, NR, B_GROUPS * B_DH])
        mask_b = sb("mask_b", [P, NR * SEQ + 2 * P])
        probs_b = sb("probs_b", [P, SEQ + 2 * P])
        gate_b = sb("gate_b", [P, SEQ])
        q_a = at("q_a", branch_at, [P, 2, SEQ])
        gate_a = at("gate_a", branch_at + 4096, [P, 2, SEQ])
        k_a = at("k_a", branch_at + 8192, [P, A_KV, SEQ])
        v_a = at("v_a", branch_at + 12288, [P, 4, P])
        mask_a = at("mask_a", branch_at + 14336, [P, 2 * P])
        probs_a = at("probs_a", branch_at + 15360, [P, 2, 2, 2 * P + 3])
        angle, turns = (at(n, shared_at + 2048 * k, [P, SEQ]) for k, n in enumerate(("angle", "turns")))
        rests = [at(f"rest{k}", where, [P, SEQ]) for k, where in
                 enumerate((shared_at + 2 * 2048, branch_at + 2048, branch_at + 4096, branch_at + 6144))]
        pos_row = at("pos_row", shared_at + 3 * 2048, [P, SEQ], I32)
        k_rot = at("k_rot", shared_at + 4 * 2048, [P, SEQ])
        vT_a = at("vT_a", shared_at + 5 * 2048, [P, SEQ])
        merged = at("merged", shared_at, [P, KT, SEQ])

        probsT = sb("probsT", [P, 6, P])
        out_q = sb("out_q", [P, P])
        shifted = sb("shifted", [P, SEQ])
        tables_at = top[0]
        cos_a, sin_a, cos_b, sin_b = (sb(n, [P, SEQ]) for n in ("cos_a", "sin_a", "cos_b", "sin_b"))
        part_a, part_b = at("part_a", tables_at, [P, 2, SEQ]), at("part_b", tables_at + 4096, [P, 2, SEQ])
        ident = sb("ident", [P, P])
        rope_col = sb("rope_col", [P, 4])
        gbias = sb("gbias", [P, 2 * KT])
        sink_row = sb("sink_row", [P, A_HEADS])
        sink_pair = sb("sink_pair", [P, A_HEADS, 2])
        rowmax, negmax = sb("rowmax", [P, 2, 2]), sb("negmax", [P, 2, 2])
        denom, rdenom = sb("denom", [P, 2, 2]), sb("rdenom", [P, 2, 2])
        stats = sb("stats", [P, NR, O_ITERS, 6])
        variance, root, correction = sb("variance", [P, NR]), sb("root", [P, NR]), sb("correction", [P, NR])
        meanvar, rstd, shift = sb("meanvar", [P, NR, 2]), sb("rstd", [P, NR]), sb("shift", [P, NR])

        acc = [ctx.enter_context(nc.psum_tensor(f"acc{b}", [P, SEQ], F32)) for b in range(4)]
        ps_scores = ctx.enter_context(nc.psum_tensor("ps_scores", [P, 2 * SEQ], F32))
        ps_turn = ctx.enter_context(nc.psum_tensor("ps_turn", [P, SEQ], F32))
        ps_out = ctx.enter_context(nc.psum_tensor("ps_out", [P, SEQ], F32))

        raw_in = [sem(f"raw_in{s}") for s in range(RING)]
        x_lo_done, kv_full, k_read = sem("x_lo_done"), sem("kv_full"), sem("k_read")
        hi_done, lo_done, slot_used = sem("hi_done"), sem("lo_done"), sem("slot_used")
        full, free = [sem(f"full{b}") for b in range(4)], [sem(f"free{b}") for b in range(4)]
        small_in, mask_b_in_sem, row_in, store = sem("small_in"), sem("mask_b_loaded"), sem("row_in"), sem("store")
        x_in = [sem(f"x_in{r}") for r in range(NR)]
        pos_in = sem("pos_in")
        ident_step, table_step, table_arg, table_done = sem("ident_step"), sem("table_step"), sem("table_arg"), sem("table_done")
        sink_step, sink_set = sem("sink_step"), sem("sink_set")
        rope_parts, rope_done = sem("rope_parts"), sem("rope_done")
        v_out, v_turned, v_a_ready = sem("v_out"), sem("v_turned"), sem("v_a_ready")
        sig_ready = sem("sig_ready")
        masked_ready = sem("masked_ready")
        scores_ready, rowmax_ready, negmax_ready = sem("scores_ready"), sem("rowmax_ready"), sem("negmax_ready")
        probs_ready, probsT_psum, probsT_ready = sem("probs_ready"), sem("probsT_psum"), sem("probsT_ready")
        probsT_tail, recip_ready, out_psum = sem("probsT_tail"), sem("recip_ready"), sem("out_psum")
        out_scaled, outT_psum, outT_used = sem("out_scaled"), sem("outT_psum"), sem("outT_used")
        og_hi_ready, og_ready = sem("og_hi_ready"), sem("og_ready")
        merge_sig, merged_ready = sem("merge_sig"), sem("merged_ready")
        merged_hi_ready, merged_lo_ready = sem("merged_hi_ready"), sem("merged_lo_ready")
        var_ready, root_ready = sem("var_ready"), sem("root_ready")
        stats_ready, ln_step, centred, scaled, finished = (sem("stats_ready"), sem("ln_step"), sem("centred"),
                                                           sem("scaled"), sem("finished"))

        w_in_v = w_in.rearrange("(k p) c -> p k c", p=P)
        w_pa_v = w_pa.rearrange("(k p) c -> p k c", p=P)
        w_pb_v = w_pb.rearrange("(k p) c -> p k c", p=P)
        w_out_v = w_out.rearrange("(k p) c -> p k c", p=P)
        xT_v = xT.rearrange("(k p) s -> p k s", p=P)
        x_v = x.rearrange("(j r) d -> r j d", r=NR)
        out_v = out.rearrange("b (j r) d -> r (b j) d", r=NR)

        def by_block(t):
            return t.rearrange("p (b r j) -> p r b j", b=4, r=NR)

        def by_residue(t):
            return t.rearrange("p (r b j) -> p r b j", b=4, r=NR)

        block = ctx.enter_context(nc.Block())

        @block.sync
        def _(sp):
            def job(n, first, off, pieces):
                slot = off % RING
                loads = reversed(list(pieces(raw[:, slot, :])))
                if not first:
                    sp.wait_ge(lo_done, n + (off - RING + 1 - PRO_JOBS + 4))
                for dst, src in loads:
                    sp.dma_start(dst, src).then_inc(raw_in[slot], 16)

            def wait_split(n):
                m, part = divmod(n, 3)
                if part == 0:
                    sp.wait_ge(lo_done, m + 1)
                else:
                    sp.wait_ge(x_lo_done, 2 * m + part)

            def halves(dst, src):
                return [(dst[h:h + P // 2], src[h:h + P // 2]) for h in (0, P // 2)]

            def load_a(i, q):
                def pieces(t):
                    for half, col in enumerate((QA, GA)):
                        for k in range(2):
                            c = 512 * half + 256 * k
                            src = w_in_v[:, 2 * q + k, col:col + A_WIDTH].rearrange("p (v c) -> p v c", v=A_KV)
                            yield (t[:, c:c + 256].rearrange("p (v c) -> p v c", v=A_KV), src[:, :, bass.ds(i * P, P)])
                return pieces

            def load_b(h, g, q):
                def pieces(t):
                    col = (QB, KB, VB)[g]
                    for k in range(2):
                        c = (512 if g == 1 else 384) * k
                        src = w_in_v[:, 2 * q + k, col:col + B_GROUPS * GW].rearrange("p (g c) -> p g c", g=B_GROUPS)
                        dst = t[:, c:c + 384].rearrange("p (g c) -> p g c", g=B_GROUPS)
                        if g == 1:
                            yield dst, src[:, :, bass.ds(h * P, P)]
                            yield t[:, c + 384:c + 512], w_in_v[:, 2 * q + k, GB:GB + GW][:, bass.ds(h * P, P)]
                        else:
                            yield from halves(dst, src[:, :, bass.ds(h * P, P)])
                return pieces

            def load_m(n, g, q):
                def pieces(t):
                    cols = bass.ds(n * 256, 256)
                    for k in range(4):
                        if g < 2:
                            yield (t[:, 256 * k:256 * k + 256],
                                   w_in_v[:, 4 * q + k, MG + D * g:MG + D * (g + 1)][:, cols])
                        elif g == 2:
                            yield t[:, 256 * k:256 * k + 256], w_pa_v[:, 4 * q + k, cols]
                        elif k < 2:
                            yield from halves(t[:, 256 * k:256 * k + 256], w_pb_v[:, 2 * q + k, cols])
                return pieces

            def load_o(n, q):
                return lambda t: [part for k in range(2)
                                  for part in halves(t[:, 512 * k:512 * k + 512], w_out_v[:, 2 * q + k, bass.ds(n * 512, 512)])]

            for n in range(PRO_JOBS):
                m, part = divmod(n, 3)
                slot = n % RING
                if n >= RING:
                    wait_split(n - RING)
                if part == 0:
                    sp.dma_start(raw[:, slot, :].rearrange("p (k c) -> p k c", k=4), w_in_v[:, 4 * m:4 * m + 4, KA:GA])\
                        .then_inc(raw_in[slot], 16)
                else:
                    k = 4 * m + 2 * (part - 1)
                    sp.dma_start(raw[:, slot, :].rearrange("p (k c) -> p k c", k=2), xT_v[:, k:k + 2, :])\
                        .then_inc(raw_in[slot], 16)
                if n == 2:
                    sp.dma_start(rope_col[:], rope_rows).then_inc(pos_in, 16)
                    sp.dma_start(pos_row[:], pos.partition_broadcast(P)).then_inc(pos_in, 16)
            for q in range(RING):
                wait_split(PRO_JOBS - RING + q)
                job(None, True, q, load_a(0, q))
            sp.dma_start(mask_a[:], mask_a_in).then_inc(small_in, 16)
            sp.dma_start(sink_row[:], sinks.partition_broadcast(P)).then_inc(small_in, 16)
            sp.dma_start(gbias[:], gate_bias).then_inc(small_in, 16)

            def iter_a(i, done):
                for q in range(done, A_JOBS):
                    job(job_a(i), False, q, load_a(i, q))

            def iter_b(h, first):
                for k in range(B_JOBS):
                    job(job_b(h), False, k, load_b(h, k // 8, k % 8))
                    if first and k == 15:
                        sp.wait_ge(og_ready, 2 * A_ITERS)
                        sp.dma_start(mask_b[:], mask_b_in).then_inc(mask_b_in_sem, 16)

            def iter_m(n):
                for k in range(M_JOBS):
                    g, q = ((0, k) if k < 4 else (1, k - 4) if k < 8 else (2, k - 8) if k < 10 else (3, k - 10))
                    job(job_m(n), False, k, load_m(n, g, q))

            def iter_o(n, first):
                for q in range(O_JOBS):
                    job(job_o(n), False, q, load_o(n, q))
                    if first and q == 4:
                        sp.wait_ge(full[3], fills_m(3, M_ITERS))
                    if first and q >= 4:
                        sp.dma_start(z[:, q - 4, :], x_v[q - 4]).then_inc(x_in[q - 4], 16)
                if first:
                    sp.dma_start(g_row[:], ln_g.partition_broadcast(P)).then_inc(row_in, 16)
                    sp.dma_start(b_row[:], ln_b.partition_broadcast(P)).then_inc(row_in, 16)

            iter_a(0, RING)
            with sp.Fori(1, A_ITERS) as i:
                iter_a(i, 0)
            iter_b(0, True)
            with sp.Fori(1, B_HEADS) as h:
                iter_b(h, False)
            with sp.Fori(0, M_ITERS) as n:
                iter_m(n)
            iter_o(0, True)
            with sp.Fori(1, O_ITERS) as n:
                iter_o(n, False)
            for r in range(NR):
                sp.wait_ge(scaled, 2 * r + 2)
                sp.dma_start(out_v[r, :, 0:LN_SPLIT], z[:, r, 0:LN_SPLIT]).then_inc(store, 16)
                sp.wait_ge(finished, 2 * r + 2)
                sp.dma_start(out_v[r, :, LN_SPLIT:D], z[:, r, LN_SPLIT:D]).then_inc(store, 16)
            sp.wait_ge(store, 32 * NR)

        @block.gpsimd
        def _(pool):
            nc.gpsimd.memset(ident[:], 0.0).then_inc(ident_step, 1)
            pool.wait_ge(ident_step, 1)
            nc.gpsimd.affine_select(out=ident[:], in_=ident[:], compare_op=ALU.not_equal, fill=1.0, base=0,
                                    pattern=[[-1, P]], channel_multiplier=1).then_inc(ident_step, 1)

            def low(dst, slot, hi, n):
                pool.wait_ge(hi_done, n + 1)
                nc.gpsimd.tensor_tensor(dst, raw[:, slot, :], hi.bitcast(F32), ALU.subtract).then_inc(lo_done, 1)

            for m in range(4):
                low(w_lo[:, m, :], 3 * m % RING, w_hi[:, m, :], 3 * m)
            with pool.Fori(0, (job_o(O_ITERS) - PRO_JOBS) // RING) as i:
                for s in range(RING):
                    low(w_lo[:, s, :], s, w_hi[:, s, :], i * RING + (PRO_JOBS + s))
            pool.wait_ge(row_in, 32)
            for r in range(NR):
                columns = z[:, r, LN_SPLIT:D]
                pool.wait_ge(centred, r + 1)
                nc.gpsimd.tensor_tensor(columns, columns, g_row[:, LN_SPLIT:D], ALU.mult).then_inc(finished, 1)
                pool.wait_ge(finished, 2 * r + 1)
                nc.gpsimd.tensor_tensor(columns, columns, b_row[:, LN_SPLIT:D], ALU.add).then_inc(finished, 1)

        @block.scalar
        def _(act):
            def high(n, off):
                s = off % RING
                act.wait_ge(raw_in[s], n * (16 * LOADS // RING) +
                            (16 * LOADS * (off // RING + 1) - 16 * (LOADS - 1) * PRO_JOBS // RING))
                act.wait_ge(slot_used, n + (off - 2 * RING - RING + 1))
                nc.scalar.activation(w_hi[:, s, :], raw[:, s, :], ACT.Copy).then_inc(hi_done, 1)

            def exps_a(u, a):
                b, j = divmod(u, 2)
                lo = P if b == 0 else 0
                act.wait_ge(negmax_ready, a + 1)
                for hh in range(2):
                    s = probs_a[:, j, hh, lo:2 * P + 1]
                    e = nc.scalar.activation(s, s, ACT.Exp, bias=negmax[:, j, hh:hh + 1], scale=A_SCALE,
                                             accum_out=denom[:, j, hh:hh + 1])
                e.then_inc(probs_ready, 1)

            def exps_b(u, a):
                act.wait_ge(negmax_ready, a + 1)
                nc.scalar.activation(probs_b[:], probs_b[:], ACT.Exp, bias=negmax[:, u % 2, 0:1], scale=B_SCALE,
                                     accum_out=denom[:, u % 2, 0:1]).then_inc(probs_ready, 1)

            def probs_out(kind, u, a):
                act.wait_ge(probsT_psum, a + 1)
                if kind == "b" or u:
                    act.wait_ge(out_psum, a)
                dst, src = probsT[:, 0:4, :], ps_turn.rearrange("p (c q) -> p c q", c=4)
                if kind == "a" and u < 2:
                    dst, src = (t.rearrange("p (v k) q -> p v k q", v=2)[:, :, 1, :] for t in (dst, src))
                nc.scalar.activation(dst, src, ACT.Copy).then_inc(probsT_ready, 1)

            def attend(kind, plan, g, first_unit):
                for stage, u in plan.get(g, ()):
                    if stage == "scores":
                        (exps_a if kind == "a" else exps_b)(u, first_unit + u)
                    if stage == "turn_probs":
                        probs_out(kind, u, first_unit + u)

            for n in range(PRO_JOBS):
                m, part = divmod(n, 3)
                act.wait_ge(raw_in[n % RING], 16 * (n // RING + 1))
                k = 4 * m + 2 * (part - 1)
                dst = w_hi[:, m, :] if part == 0 else x_hi[:, k:k + 2, :].rearrange("p k c -> p (k c)")
                nc.scalar.activation(dst, raw[:, n % RING, :], ACT.Copy).then_inc(hi_done, 1)
            for off in range(AHEAD):
                high(job_a(0), off)

            def sines(k):
                table, col = ((cos_a, None), (sin_a, 3), (cos_b, None), (sin_b, 1))[k]
                act.wait_ge(table_arg, k + 1)
                scale = 1.0 if col is None else rope_col[:, col:col + 1]
                nc.scalar.activation(table[:], rests[k][:], ACT.Sin, scale=scale).then_inc(table_done, 1)

            def iter_a(i, with_attention):
                for g, (job, _, _, bank, _, last, opens, _) in enumerate(A_BLOCKS):
                    if opens:
                        high(job_a(i), job + AHEAD)
                    if with_attention:
                        attend("a", A_PLAN, g, unit_a(i - 1))
                    if not with_attention and g == 2:
                        act.wait_ge(kv_full, 2)
                        nc.scalar.activation(by_block(vT_a[:]), by_residue(ps_out[:]), ACT.Copy).then_inc(v_out, 1)
                    if not with_attention and g in (13, 21):
                        for k in (0, 1) if g == 13 else (2, 3):
                            sines(k)
                    if not with_attention and g == 10:
                        act.wait_ge(v_turned, 1)
                        nc.scalar.activation(v_a[:], ps_turn.rearrange("p (b c) -> p b c", b=4), ACT.Copy)\
                            .then_inc(v_a_ready, 1)
                    if last and bank >= 2:
                        act.wait_ge(full[bank], fills_a(bank, i) + 1)
                        if not with_attention and bank == 2:
                            act.wait_ge(table_done, 4)
                        if with_attention and bank == 2:
                            act.wait_ge(og_ready, i * 2)
                        nc.scalar.activation(by_block(gate_a[:, bank - 2, :]), by_residue(acc[bank][:]), ACT.Sigmoid)\
                            .then_inc(sig_ready, 1)

            def iter_b(h, first):
                for g, (job, group, _, bank, _, last, opens, _) in enumerate(B_BLOCKS):
                    if opens:
                        high(job_b(h), job + AHEAD)
                    if first:
                        attend("a", A_PLAN, g, unit_a(A_ITERS - 1))
                    else:
                        attend("b", B_PLAN, g, unit_b(h - 1))
                    if last and group == 1 and bank == 3:
                        act.wait_ge(full[3], fills_b(3, h) + 1)
                        act.wait_ge(og_ready, h + 2 * A_ITERS)
                        nc.scalar.activation(gate_b[:], acc[3][:], ACT.Sigmoid).then_inc(sig_ready, 1)
                    if last and group == 2:
                        act.wait_ge(full[bank], fills_b(bank, h) + (3 if bank < 3 else 2))
                        act.wait_ge(out_psum, unit_b(h))
                        nc.scalar.activation(v_b[:, bank, :], acc[bank][:, 0:384], ACT.Copy).then_inc(free[bank], 1)

            def iter_m(n, first, last_iter):
                for g, (job, group, _, bank, _, last, opens, _) in enumerate(M_BLOCKS):
                    if opens:
                        high(job_m(n), job + AHEAD)
                    if first:
                        attend("b", B_PLAN_MERGE, g, unit_b(B_HEADS - 1))
                    if last and group < 2:
                        act.wait_ge(full[bank], fills_m(bank, n) + 1)
                        if not first and bank % 2 == 0:
                            act.wait_ge(merged_ready, n * 2)
                        part, t = (part_a, part_b)[group], bank % 2
                        nc.scalar.activation(part[:, t, :], acc[bank][:], ACT.Sigmoid,
                                             bias=gbias[:, bass.ds(n * 2 + (KT * group + t), 1)]).then_inc(merge_sig, 1)
                    if last_iter and group == 2 and job == 8 and bank == 1:
                        merged_high(0, 4, 12)
                        merged_high(4, 8, 12)
                    if last_iter and group == 2 and job == 9 and bank == 1:
                        merged_high(8, 12, 12)
                        merged_high(12, 14, 14)

            def merged_high(lo, hi, ready):
                act.wait_ge(merged_ready, ready)
                act.wait_ge(full[3], fills_m(3, M_ITERS - 1) + 1)
                nc.scalar.activation(x_hi[:, lo:hi, :], merged[:, lo:hi, :], ACT.Copy).then_inc(merged_hi_ready, 1)

            def iter_o(n, last_iter):
                for g, (job, _, _, bank, _, last, opens, _) in enumerate(O_BLOCKS):
                    if opens and not (last_iter and job + AHEAD >= O_JOBS):
                        high(job_o(n), job + AHEAD)

            iter_a(0, False)
            with act.Fori(1, A_ITERS) as i:
                iter_a(i, True)
            iter_b(0, True)
            with act.Fori(1, B_HEADS) as h:
                iter_b(h, False)
            iter_m(0, True, False)
            with act.Fori(1, M_ITERS - 1) as n:
                iter_m(n, False, False)
            iter_m(M_ITERS - 1, False, True)
            merged_high(14, 16, 16)
            with act.Fori(0, O_ITERS - 1) as n:
                iter_o(n, False)
            iter_o(O_ITERS - 1, True)
            for r in range(NR):
                act.wait_ge(var_ready, r + 1)
                nc.scalar.activation(root[:, r:r + 1], variance[:, r:r + 1], ACT.Sqrt).then_inc(root_ready, 1)
                act.wait_ge(ln_step, 6 * r + 6)
                columns = z[:, r, LN_SPLIT:D]
                nc.scalar.activation(columns, columns, ACT.Identity, bias=shift[:, r:r + 1],
                                     scale=rstd[:, r:r + 1]).then_inc(centred, 1)

        @block.vector
        def _(dve):
            step = [0]

            def chain(instruction):
                step[0] += 1
                instruction.then_inc(table_step, 1)
                dve.wait_ge(table_step, step[0])

            two_pi = 6.283185307179586
            c1 = 6.28125
            c2 = 0.0019350051879882812
            c3 = two_pi - c1 - c2
            magic = 1.5 * 2.0 ** 23
            pi = 3.141592

            def reduce_angle(dst, src, unit, offset):
                chain(nc.vector.tensor_scalar(turns[:], src, 1.0 / (two_pi * unit), offset, ALU.mult, ALU.add))
                chain(nc.vector.tensor_scalar(turns[:], turns[:], magic, -magic, ALU.add, ALU.add))
                for k, c in enumerate((c1, c2, c3)):
                    chain(nc.vector.scalar_tensor_tensor(dst, turns[:], -c * unit, src if k == 0 else dst,
                                                         ALU.mult, ALU.add))

            def x_low(e):
                n = 3 * (e // 2) + 1 + e % 2
                dve.wait_ge(hi_done, n + 1)
                lo, hi = (t[:, 2 * e:2 * e + 2, :].rearrange("p k c -> p (k c)") for t in (x_lo, x_hi))
                nc.vector.tensor_tensor(lo, raw[:, n % RING, :], hi.bitcast(F32), ALU.subtract).then_inc(x_lo_done, 1)

            for e in range(8):
                x_low(e)
            dve.wait_ge(pos_in, 32)
            for k, (freq, quarter) in enumerate(((2, True), (2, False), (0, True), (0, False))):
                rest = rests[k]
                if quarter:
                    chain(nc.vector.tensor_copy(angle[:], pos_row[:]))
                    chain(nc.vector.tensor_scalar(angle[:], angle[:], rope_col[:, freq:freq + 1], None, ALU.mult))
                    reduce_angle(angle[:], angle[:], 65536.0, 0.0)
                reduce_angle(rest[:], angle[:], 1.0, 0.25 if quarter else 0.0)
                chain(nc.vector.tensor_scalar(rest[:], rest[:], two_pi / 4 if quarter else 0.0, -pi, ALU.add, ALU.max))
                nc.vector.tensor_scalar(rest[:], rest[:], pi, None, ALU.min).then_inc(table_arg, 1)
            dve.wait_ge(small_in, 48)
            nc.vector.tensor_scalar(sink_pair[:, :, 0], sink_row[:], 1.0 / A_SCALE, None, ALU.mult).then_inc(sink_step, 1)
            nc.vector.tensor_scalar(sink_pair[:, :, 1], sink_row[:], -1.0, None, ALU.mult).then_inc(sink_step, 1)
            dve.wait_ge(sink_step, 2)
            dve.wait_ge(table_done, 2)

            def rope(dst, src, src_full, src_free, filled, done, parts_done, half, cos, sin):
                dve.wait_ge(src_full, filled)
                dve.wait_ge(rope_done, done)
                to_order, from_order = (by_block, by_residue) if half == 32 else (lambda t: t, lambda t: t)
                nc.vector.tensor_tensor(to_order(dst), from_order(src[:]), from_order(cos[:]), ALU.mult)\
                    .then_inc(rope_parts, 1)
                parts = P // half
                for k in range(parts):
                    to, frm = slice(half * k, half * (k + 1)), slice(half * (k ^ 1), half * ((k ^ 1) + 1))
                    last = nc.vector.tensor_tensor(to_order(shifted[to, :]), from_order(src[frm, :]),
                                                   from_order(sin[frm, :]), ALU.mult)
                    last.then_inc(src_free if k == parts - 1 else rope_parts, 1)
                dve.wait_ge(rope_parts, parts_done)
                dve.wait_ge(src_free, filled)
                nc.vector.tensor_tensor(dst, dst, shifted[:], ALU.add).then_inc(rope_done, 1)

            parts_a, parts_b = 4, 2

            def mask_max_a(u, a):
                b, j = divmod(u, 2)
                lo = P if b == 0 else 0
                dve.wait_ge(scores_ready, a + 1)
                if u >= 2:
                    dve.wait_ge(probsT_psum, a - 1)
                nc.vector.tensor_copy(probs_a[:, j, :, 2 * P:2 * P + 1], probs_a[:, j, :, 2 * P + 1:2 * P + 2])
                masked = probs_a[:, j, :, lo:2 * P]
                nc.vector.tensor_tensor(masked, ps_scores[:].rearrange("p (h k) -> p h k", h=2)[:, :, lo:2 * P],
                                        mask_a[:, lo:2 * P].unsqueeze(1).to_broadcast([P, 2, 2 * P - lo]), ALU.add)\
                    .then_inc(masked_ready, 1)
                dve.wait_ge(masked_ready, a + 1)
                nc.vector.tensor_reduce(rowmax[:, j, :], masked, mybir.AxisListType.X, ALU.max).then_inc(rowmax_ready, 1)
                dve.wait_ge(rowmax_ready, a + 1)
                nc.vector.scalar_tensor_tensor(negmax[:, j, :], rowmax[:, j, :], -A_SCALE, probs_a[:, j, :, 2 * P + 2],
                                               ALU.mult, ALU.min).then_inc(negmax_ready, 1)

            def mask_max_b(u, a):
                dve.wait_ge(scores_ready, a + 1)
                dve.wait_ge(probsT_psum, a)
                nc.vector.tensor_tensor(probs_b[:, 0:SEQ], ps_scores[:, 0:SEQ], mask_b[:, u * SEQ:(u + 1) * SEQ], ALU.add)
                nc.vector.tensor_tensor(probs_b[:, SEQ:SEQ + 2 * P], ps_scores[:, SEQ:SEQ + 2 * P],
                                        mask_b[:, NR * SEQ:NR * SEQ + 2 * P], ALU.add).then_inc(masked_ready, 1)
                dve.wait_ge(masked_ready, a + 1)
                nc.vector.tensor_reduce(rowmax[:, u % 2, 0:1], probs_b[:], mybir.AxisListType.X, ALU.max)\
                    .then_inc(rowmax_ready, 1)
                dve.wait_ge(rowmax_ready, a + 1)
                nc.vector.tensor_scalar(negmax[:, u % 2, 0:1], rowmax[:, u % 2, 0:1], -B_SCALE, None, ALU.mult)\
                    .then_inc(negmax_ready, 1)

            def probs_tail(u, a, h):
                dve.wait_ge(probsT_psum, a + 1)
                dve.wait_ge(out_psum, a)
                nc.vector.tensor_copy(probsT[:, 4:6, :], ps_scores[:, SEQ + 2 * P:2 * SEQ].rearrange("p (c q) -> p c q", c=2))\
                    .then_inc(probsT_tail, 1)

            def scale_out(kind, u, a):
                j = u % 2
                dve.wait_ge(probs_ready, a + 1)
                n = 2 if kind == "a" else 1
                nc.vector.reciprocal(rdenom[:, j, 0:n], denom[:, j, 0:n]).then_inc(recip_ready, 1)
                dve.wait_ge(out_psum, a + 1)
                dve.wait_ge(recip_ready, a + 1)
                if kind == "a":
                    shape = [P, 2, A_DH]
                    nc.vector.tensor_tensor(out_q[:].rearrange("p (h d) -> p h d", h=2),
                                            ps_out[:, 0:P].rearrange("p (h d) -> p h d", h=2),
                                            rdenom[:, j, :].unsqueeze(2).to_broadcast(shape), ALU.mult)\
                        .then_inc(out_scaled, 1)
                else:
                    nc.vector.tensor_scalar(out_q[:], ps_out[:, 0:P], rdenom[:, j, 0:1], None, ALU.mult)\
                        .then_inc(out_scaled, 1)

            def split_gated(kind, gated, tile, done):
                hi, lo = (t[:, bass.ds(tile, 1), :].rearrange("p t s -> p (t s)") for t in (og_hi, og_lo))
                if kind == "a":
                    hi, lo, gated = by_residue(hi), by_residue(lo), by_block(gated)
                nc.vector.tensor_copy(hi, gated).then_inc(og_hi_ready, 1)
                dve.wait_ge(og_hi_ready, done + 1)
                nc.vector.tensor_tensor(lo, gated, hi.bitcast(F32), ALU.subtract).then_inc(og_ready, 1)

            def gate_out(kind, u, a, i):
                dve.wait_ge(outT_psum, a + 1)
                b, j = divmod(u, 2)
                g = gate_a[:, j, b * P:(b + 1) * P] if kind == "a" else gate_b[:, u * P:(u + 1) * P]
                nc.vector.tensor_tensor(g, ps_out[:, P:2 * P], g, ALU.mult).then_inc(outT_used, 1)
                if kind == "a" and b == 3:
                    dve.wait_ge(outT_used, a + 1)
                    split_gated(kind, gate_a[:, j, :], i + A_ITERS * j, i * 2 + j)
                if kind == "b" and u == 3:
                    dve.wait_ge(outT_used, a + 1)
                    split_gated(kind, gate_b[:], i + 2 * A_ITERS, i + 2 * A_ITERS)

            def attend(kind, plan, g, first_unit, i):
                if kind == "a" and g == 0:
                    nc.vector.tensor_copy(probs_a[:, :, :, 2 * P + 1:2 * P + 3].rearrange("p j v c -> p (j v) c"),
                                          sink_pair[:, bass.ds(i * 4, 4), :]).then_inc(sink_set, 1)
                    dve.wait_ge(sink_set, i + 1)
                if kind == "b" and g == 0:
                    dve.wait_ge(mask_b_in_sem, 16)
                for stage, u in plan.get(g, ()):
                    a = first_unit + u
                    if stage == "scores":
                        (mask_max_a if kind == "a" else mask_max_b)(u, a)
                    elif stage == "turn_probs" and kind == "b":
                        probs_tail(u, a, i)
                    elif stage == "values":
                        scale_out(kind, u, a)
                    elif stage == "turn_out":
                        gate_out(kind, u, a, i)

            def gate(dst, src, bank, done):
                dve.wait_ge(sig_ready, done + 1)
                nc.vector.tensor_tensor(dst, src, dst, ALU.mult).then_inc(free[bank], 1)

            rope(k_rot[:], ps_scores[:, 0:SEQ], kv_full, k_read, 1, 0, parts_a, 32, cos_a, sin_a)
            dve.wait_ge(rope_done, 1)
            for kv in range(A_KV):
                for hh in range(2):
                    nc.vector.tensor_copy(k_a[A_DH * hh:A_DH * hh + A_DH, kv, :], k_rot[A_DH * kv:A_DH * kv + A_DH, :])\
                        .then_inc(rope_done, 1)

            def iter_a(i, with_attention):
                for g, (job, _, _, bank, _, last, opens, _) in enumerate(A_BLOCKS):
                    if with_attention:
                        attend("a", A_PLAN, g, unit_a(i - 1), i - 1)
                    if last and bank < 2:
                        if with_attention and bank == 0:
                            dve.wait_ge(scores_ready, unit_a(i))
                        rope(q_a[:, bank, :], acc[bank], full[bank], free[bank], fills_a(bank, i) + 1, i * 2 + (5 + bank),
                             i * (2 * parts_a) + parts_a * (bank + 2), 32, cos_a, sin_a)
                    elif last:
                        gate(by_block(gate_a[:, bank - 2, :]), by_residue(acc[bank][:]), bank, i * 2 + (bank - 2))

            all_a = parts_a * (1 + 2 * A_ITERS)

            def iter_b(h, first):
                for g, (job, group, _, bank, _, last, opens, _) in enumerate(B_BLOCKS):
                    if first:
                        attend("a", A_PLAN, g, unit_a(A_ITERS - 1), A_ITERS - 1)
                    else:
                        attend("b", B_PLAN, g, unit_b(h - 1), h - 1)
                    if last and group < 2 and bank < 3:
                        if not first and group == 0 and bank == 0:
                            dve.wait_ge(scores_ready, unit_b(h))
                        tile = h * (6 * parts_b) + (all_a + parts_b * (3 * group + bank + 1))
                        rope((q_b, k_b)[group][:, bank, :], acc[bank], full[bank], free[bank], fills_b(bank, h) + (group + 1),
                             h * 6 + (5 + 2 * A_ITERS + 3 * group + bank), tile, 64, cos_b, sin_b)
                    if last and group == 1 and bank == 3:
                        gate(gate_b[:], acc[3][:], 3, h + 2 * A_ITERS)

            def iter_m(n, first):
                for g, (job, group, _, bank, _, last, opens, _) in enumerate(M_BLOCKS):
                    if first:
                        attend("b", B_PLAN_MERGE, g, unit_b(B_HEADS - 1), B_HEADS - 1)
                    if last and group < 2:
                        dve.wait_ge(merge_sig, n * 4 + (2 * group + bank % 2 + 1))
                        dve.sem_inc(free[bank], 1)
                    if last and group >= 2:
                        t = bank % 2
                        part = (part_a, part_b)[group - 2]
                        dve.wait_ge(full[bank], fills_m(bank, n) + 2)
                        nc.vector.tensor_tensor(part[:, t, :], acc[bank][:], part[:, t, :], ALU.mult)\
                            .then_inc(free[bank], 1)
                        if group == 3:
                            dve.wait_ge(free[bank], fills_m(bank, n) + 2)
                            dve.wait_ge(free[t], fills_m(t, n) + 2)
                            nc.vector.tensor_tensor(merged[:, bass.ds(n * 2 + t, 1), :].rearrange("p k c -> p (k c)"),
                                                    part_a[:, t, :], part_b[:, t, :], ALU.add).then_inc(merged_ready, 1)
                    if isinstance(n, int) and n == M_ITERS - 1 and group == 3 and job == 10 and bank == 3:
                        for c in range(3):
                            merged_low(4 * c, 4 * c + 4, c + 1)
                        merged_low(12, 14, 4)

            def merged_low(lo, hi, ready):
                dve.wait_ge(merged_hi_ready, ready)
                nc.vector.tensor_tensor(x_lo[:, lo:hi, :], merged[:, lo:hi, :], x_hi[:, lo:hi, :].bitcast(F32),
                                        ALU.subtract).then_inc(merged_lo_ready, 1)

            def iter_o(n, last_iter):
                for r in range(NR):
                    dve.wait_ge(full[r], fills_o(r, n) + 1)
                    if isinstance(n, int) and n == 0:
                        dve.wait_ge(x_in[r], 16)
                    chunk = z[:, r, bass.ds(n * SEQ, SEQ)]
                    nc.vector.scalar_tensor_tensor(chunk, chunk, ALPHA, acc[r][:], ALU.mult, ALU.add)\
                        .then_inc(free[r], 1)
                    dve.wait_ge(free[r], fills_o(r, n) + 1)
                    nc.vector.bn_stats(stats[:, r, bass.ds(n, 1), :].rearrange("p n s -> p (n s)"), chunk)\
                        .then_inc(stats_ready, 1)
                    if not last_iter:
                        continue
                    dve.wait_ge(stats_ready, NR * n + r + 1)
                    nc.vector.bn_aggr(meanvar[:, r, :], stats[:, r, :, :].rearrange("p n s -> p (n s)"))\
                        .then_inc(ln_step, 1)
                    dve.wait_ge(ln_step, 6 * r + 1)
                    var, inv, cor = variance[:, r:r + 1], rstd[:, r:r + 1], correction[:, r:r + 1]
                    nc.vector.tensor_scalar(var, meanvar[:, r, 1:2], EPS, None, ALU.add).then_inc(var_ready, 1)
                    dve.wait_ge(root_ready, r + 1)
                    nc.vector.reciprocal(inv, root[:, r:r + 1]).then_inc(ln_step, 1)
                    dve.wait_ge(ln_step, 6 * r + 2)
                    nc.vector.tensor_scalar(cor, inv, inv, var, ALU.mult, ALU.mult).then_inc(ln_step, 1)
                    dve.wait_ge(ln_step, 6 * r + 3)
                    nc.vector.tensor_scalar(cor, cor, -0.5, 1.5, ALU.mult, ALU.add).then_inc(ln_step, 1)
                    dve.wait_ge(ln_step, 6 * r + 4)
                    nc.vector.tensor_scalar(inv, inv, cor, None, ALU.mult).then_inc(ln_step, 1)
                    dve.wait_ge(ln_step, 6 * r + 5)
                    nc.vector.tensor_scalar(shift[:, r:r + 1], meanvar[:, r, 0:1], inv, -1.0,
                                            ALU.mult, ALU.mult).then_inc(ln_step, 1)
                    if r == 0:
                        dve.wait_ge(row_in, 32)
                    columns = z[:, r, 0:LN_SPLIT]
                    nc.vector.scalar_tensor_tensor(columns, columns, meanvar[:, r, 0:1], g_row[:, 0:LN_SPLIT],
                                                   ALU.subtract, ALU.mult).then_inc(scaled, 1)
                    dve.wait_ge(scaled, 2 * r + 1)
                    nc.vector.scalar_tensor_tensor(columns, columns, inv, b_row[:, 0:LN_SPLIT],
                                                   ALU.mult, ALU.add).then_inc(scaled, 1)

            iter_a(0, False)
            with dve.Fori(1, A_ITERS) as i:
                iter_a(i, True)
            dve.wait_ge(table_done, 4)
            iter_b(0, True)
            with dve.Fori(1, B_HEADS) as h:
                iter_b(h, False)
            iter_m(0, True)
            with dve.Fori(1, M_ITERS - 1) as n:
                iter_m(n, False)
            iter_m(M_ITERS - 1, False)
            merged_low(14, 16, 5)
            iter_o(0, False)
            with dve.Fori(1, O_ITERS - 1) as n:
                iter_o(n, False)
            iter_o(O_ITERS - 1, True)

        @block.tensor
        def _(pe):
            started = [False]

            def products(into, is_full, pairs, cols, start, stop, released):
                n = 3 * len(pairs)
                k = 0
                for s_hi, s_lo, m_hi, m_lo in pairs:
                    for s, m in ((s_hi, m_hi), (s_hi, m_lo), (s_lo, m_hi)):
                        ins = nc.tensor.matmul(into[:, 0:cols], s, m, start=start and k == 0, stop=stop and k == n - 1)
                        if k == 0 and released and started[0]:
                            ins.then_inc(slot_used, 1)
                        started[0] = True
                        k += 1
                if stop:
                    ins.then_inc(is_full, 1)

            def x_moving(k):
                return x_hi[:, k, :], x_lo[:, k, :]

            def scores_a(u):
                b, j = divmod(u, 2)
                for hh in range(2):
                    rows, c = slice(A_DH * hh, A_DH * hh + A_DH), hh * SEQ
                    lo = P if b == 0 else 0
                    last = nc.tensor.matmul(ps_scores[:, c + lo:c + 2 * P], q_a[rows, j, b * P:b * P + P],
                                            k_a[rows, j, (b - 1) * P + lo:(b + 1) * P], start=True, stop=True)
                last.then_inc(scores_ready, 1)

            def scores_b(u):
                q = slice(u * P, u * P + P)
                nc.tensor.matmul(ps_scores[:, 0:SEQ], q_b[:, 0, q], k_b[:, 0, :], start=True, stop=True)
                nc.tensor.matmul(ps_scores[:, SEQ:SEQ + P], q_b[:, 1, q], k_b[:, 1, q], start=True, stop=True)
                nc.tensor.matmul(ps_scores[:, SEQ + P:SEQ + 2 * P], q_b[:, 2, q], k_b[:, 2, q], start=True, stop=True)\
                    .then_inc(scores_ready, 1)

            def attend(kind, plan, g, first_unit, i):
                for stage, u in plan.get(g, ()):
                    a = first_unit + u
                    if stage == "scores":
                        if kind == "a":
                            if u == 0:
                                pe.wait_ge(rope_done, i * 2 + 7)
                            if u:
                                pe.wait_ge(negmax_ready, a)
                            scores_a(u)
                        else:
                            if u == 0:
                                pe.wait_ge(rope_done, i * 6 + (2 * A_ITERS + 5 + 6))
                            pe.wait_ge(negmax_ready, a)
                            if not u == 0:
                                pe.wait_ge(probsT_tail, a - unit_b(0))
                            scores_b(u)
                    elif stage == "turn_probs":
                        pe.wait_ge(probs_ready, a + 1)
                        if kind == "b" or u:
                            pe.wait_ge(probsT_ready, a)
                        if kind == "a":
                            b, j = divmod(u, 2)
                            for hh in range(2):
                                for kb in ((1,) if b == 0 else (0, 1)):
                                    c = (2 * hh + kb) * P
                                    last = nc.tensor.transpose(ps_turn[:, c:c + P], probs_a[:, j, hh, kb * P:kb * P + P],
                                                               ident[:])
                        else:
                            for c in range(6):
                                dst = ps_turn[:, c * P:c * P + P] if c < 4 else ps_scores[:, (c + 2) * P:(c + 3) * P]
                                last = nc.tensor.transpose(dst, probs_b[:, c * P:c * P + P], ident[:])
                        last.then_inc(probsT_psum, 1)
                    elif stage == "values":
                        pe.wait_ge(probsT_ready, a + 1)
                        if kind == "b" or u:
                            pe.wait_ge(outT_used, a)
                        if kind == "a":
                            b, j = divmod(u, 2)
                            kbs = (1,) if b == 0 else (0, 1)
                            for hh in range(2):
                                for kb in kbs:
                                    last = nc.tensor.matmul(ps_out[:, A_DH * hh:A_DH * hh + A_DH], probsT[:, 2 * hh + kb, :],
                                                            v_a[:, b - 1 + kb, A_DH * j:A_DH * j + A_DH],
                                                            start=kb == kbs[0], stop=kb == 1)
                        else:
                            pe.wait_ge(probsT_tail, a - unit_b(0) + 1)
                            if u == 0:
                                for bank in range(4):
                                    pe.wait_ge(free[bank], fills_b(bank, i + 1))
                            for c in range(6):
                                tile, grp = (c, 0) if c < 4 else (u, c - 3)
                                last = nc.tensor.matmul(ps_out[:, 0:P], probsT[:, c, :], v_b[:, tile, grp * P:grp * P + P],
                                                        start=c == 0, stop=c == 5)
                        last.then_inc(out_psum, 1)
                    else:
                        pe.wait_ge(out_scaled, a + 1)
                        nc.tensor.transpose(ps_out[:, P:2 * P], out_q[:], ident[:]).then_inc(outT_psum, 1)

            for e in range(8):
                m = e // 2
                if e % 2 == 0:
                    pe.wait_ge(lo_done, m + 1)
                pe.wait_ge(x_lo_done, e + 1)
                for t, bank in enumerate((ps_scores[:, 0:SEQ], ps_out[:])):
                    pairs = []
                    for k in range(2):
                        c = slice(256 * (2 * (e % 2) + k) + P * t, 256 * (2 * (e % 2) + k) + P * t + P)
                        pairs.append((w_hi[:, m, c], w_lo[:, m, c], *x_moving(2 * e + k)))
                    products(bank, kv_full, pairs, SEQ, e == 0, e == 7, t == 0 and e % 2 == 0)

            def ready(n, off):
                pe.wait_ge(lo_done, n + (off + 1 - PRO_JOBS + 4))

            def iter_a(i, with_attention):
                for g, (job, _, q, bank, first, last, opens, released) in enumerate(A_BLOCKS):
                    if with_attention:
                        attend("a", A_PLAN, g, unit_a(i - 1), i - 1)
                    elif g == 8:
                        pe.wait_ge(v_out, 1)
                        pe.wait_ge(ident_step, 2)
                        for b in range(4):
                            t = nc.tensor.transpose(ps_turn[:, b * P:b * P + P], vT_a[:, b * P:b * P + P], ident[:])
                        t.then_inc(v_turned, 1)
                    if opens:
                        ready(job_a(i), job)
                    if first and with_attention:
                        pe.wait_ge(free[bank], fills_a(bank, i))
                    s, (half, j) = job % RING, divmod(bank, 2)
                    pairs = []
                    for k in range(2):
                        c = 512 * half + 256 * k + P * j
                        pairs.append((w_hi[:, s, c:c + P], w_lo[:, s, c:c + P], *x_moving(2 * q + k)))
                    products(acc[bank], full[bank], pairs, SEQ, first, last, released)

            def iter_b(h, first_iter):
                for g, (job, group, q, bank, first, last, opens, released) in enumerate(B_BLOCKS):
                    if first_iter:
                        attend("a", A_PLAN, g, unit_a(A_ITERS - 1), A_ITERS - 1)
                    else:
                        attend("b", B_PLAN, g, unit_b(h - 1), h - 1)
                    if opens:
                        ready(job_b(h), job)
                    if first:
                        pe.wait_ge(free[bank], fills_b(bank, h) + (group - (1 if bank == 3 else 0)))
                    s = job % RING
                    pairs = []
                    for k in range(2):
                        if group == 2:
                            c, r = slice(384 * k, 384 * k + 384), slice(bank * P, bank * P + P)
                            kk = 2 * q + k
                            pairs.append((x_hi[:, kk, r], x_lo[:, kk, r], w_hi[:, s, c], w_lo[:, s, c]))
                        else:
                            c = (384, 512)[group] * k + bank * P
                            pairs.append((w_hi[:, s, c:c + P], w_lo[:, s, c:c + P], *x_moving(2 * q + k)))
                    products(acc[bank], full[bank], pairs, 384 if group == 2 else SEQ, first, last, released)

            def iter_m(n, first_iter):
                for g, (job, group, q, bank, first, last, opens, released) in enumerate(M_BLOCKS):
                    if first_iter:
                        attend("b", B_PLAN_MERGE, g, unit_b(B_HEADS - 1), B_HEADS - 1)
                    if opens:
                        ready(job_m(n), job)
                    if first:
                        pe.wait_ge(free[bank], fills_m(bank, n) + group // 2)
                        if first_iter and bank % 2 == 0 and group >= 2:
                            pe.wait_ge(og_ready, (8, 12)[group - 2])
                    s, t = job % RING, bank % 2
                    pairs = []
                    for k in range(4 if group < 3 else 2):
                        c = slice(256 * k + P * t, 256 * k + P * t + P)
                        if group < 2:
                            moving = x_moving(4 * q + k)
                        else:
                            e = 4 * q + k if group == 2 else 8 + 2 * q + k
                            moving = og_hi[:, e, :], og_lo[:, e, :]
                        pairs.append((w_hi[:, s, c], w_lo[:, s, c], *moving))
                    products(acc[bank], full[bank], pairs, SEQ, first, last, released)

            def iter_o(n, first_iter, last_iter):
                for job, _, q, bank, first, last, opens, released in (O_BLOCKS_LAST if last_iter else O_BLOCKS):
                    if opens:
                        ready(job_o(n), job)
                        if first_iter:
                            pe.wait_ge(merged_lo_ready, (1, 1, 2, 2, 3, 3, 4, 5)[q])
                    if first:
                        pe.wait_ge(free[bank], fills_o(bank, n))
                    s, r = job % RING, slice(bank * P, bank * P + P)
                    pairs = [(x_hi[:, 2 * q + k, r], x_lo[:, 2 * q + k, r], w_hi[:, s, 512 * k:512 * k + 512],
                              w_lo[:, s, 512 * k:512 * k + 512]) for k in range(2)]
                    products(acc[bank], full[bank], pairs, SEQ, first, last, released)

            iter_a(0, False)
            pe.wait_ge(v_a_ready, 1)
            with pe.Fori(1, A_ITERS) as i:
                iter_a(i, True)
            iter_b(0, True)
            with pe.Fori(1, B_HEADS) as h:
                iter_b(h, False)
            iter_m(0, True)
            with pe.Fori(1, M_ITERS) as n:
                iter_m(n, False)
            iter_o(0, True, False)
            with pe.Fori(1, O_ITERS - 1) as n:
                iter_o(n, False, False)
            iter_o(O_ITERS - 1, False, True)


def kernel(x, positions, w_in, b_gate, sinks, w_pa, w_pb, w_out, ln_g, ln_b):
    import numpy as np
    import concourse.bacc as bacc
    from concourse.bass_utils import run_bass_kernel_spmd

    x, positions, w_in, b_gate, sinks, w_pa, w_pb, w_out, ln_g, ln_b = (
        np.asarray(a) for a in (x, positions, w_in, b_gate, sinks, w_pa, w_pb, w_out, ln_g, ln_b))
    t = (4 * np.arange(P)[None, :] + np.arange(NR)[:, None]).reshape(-1)

    p = np.arange(P)
    rope_rows = np.stack([10000.0 ** (-(p % 64) / 64.0), np.where(p < 64, 1.0, -1.0),
                          10000.0 ** (-(p % 32) / 32.0), np.where(p % 64 < 32, 1.0, -1.0)], axis=1).astype(np.float32)
    in_block = (4 * np.arange(32)[None, :] + np.arange(NR)[:, None]).reshape(-1)
    dist = in_block[:, None] - np.concatenate([in_block - P, in_block])[None, :]
    mask_a = np.where((dist >= 0) & (dist < 128), 0.0, MASKED).astype(np.float32)
    far = t.reshape(NR, P)[:, :, None] - t[None, None, :]
    near = np.where((far >= 0) & (far <= 128), 0.0, MASKED).transpose(1, 0, 2).reshape(P, NR * SEQ)
    step = p[:, None] - p[None, :]
    by4 = np.where(step >= 0, 0.0, MASKED)
    by16 = np.where((step >= 0) & (step % 4 == 0), 0.0, MASKED)
    mask_b = np.concatenate([near, by4, by16], axis=1).astype(np.float32)

    arrays = {
        "xT": np.ascontiguousarray(x[0].T[:, t]),
        "x": x[0],
        "pos": np.ascontiguousarray(positions[0][t]),
        "w_in": w_in[0],
        "gate_bias": np.ascontiguousarray(b_gate[0].reshape(2 * KT, P).T),
        "sinks": np.ascontiguousarray(sinks[0].reshape(A_KV, A_ITERS, 2).transpose(1, 0, 2).reshape(A_HEADS)),
        "w_pa": w_pa[0], "w_pb": w_pb[0], "w_out": w_out[0], "ln_g": ln_g[0], "ln_b": ln_b[0],
        "rope_rows": rope_rows, "mask_a": mask_a, "mask_b": mask_b,
    }
    nc = bacc.Bacc("TRN2", target_bir_lowering=False, num_devices=1)
    args = [nc.dram_tensor(n, a.shape, mybir.dt.from_np(a.dtype), kind="ExternalInput").ap() for n, a in arrays.items()]
    out = nc.dram_tensor("out", (1, SEQ, D), F32, kind="ExternalOutput").ap()
    build(nc, *args, out)
    run = run_bass_kernel_spmd(nc, [arrays], core_ids=[0])
    return run.results[0]["out"]
```

```python
from contextlib import ExitStack

import concourse.bass as bass
from concourse import mybir

F32 = mybir.dt.float32
F32R = mybir.dt.float32r
I32 = mybir.dt.int32
ALU = mybir.AluOpType
ACT = mybir.ActivationFunctionType

P = 128
SEQ = 512
D = 2048
NR = 4
KT = D // P
A_HEADS, A_KV, A_DH = 16, 2, 64
B_GROUPS, B_HEADS, B_DH = 3, 4, 128
A_WIDTH = A_HEADS * A_DH
KV_WIDTH = A_KV * A_DH
GW = B_HEADS * B_DH
QA = 0
KA = QA + A_WIDTH
GA = KA + 2 * KV_WIDTH
QB = GA + A_WIDTH
KB = QB + B_GROUPS * GW
VB = KB + B_GROUPS * GW
GB = VB + B_GROUPS * GW
MG = GB + GW
ALPHA = 2.0 ** 0.25
EPS = 1e-5
A_SCALE = A_DH ** -0.5
B_SCALE = B_DH ** -0.5
MASKED = -1.0e30

RING = 4
LOADS = 4
SLOT = 1024
PRO_JOBS = 12
A_ITERS, A_JOBS, A_UNITS = 4, 8, 8
B_JOBS, B_UNITS = 24, 4
M_ITERS, M_JOBS = 8, 12
O_ITERS, O_JOBS = 4, 8
WARM_UP = 40
AHEAD = 2


def job_a(i): return i * A_JOBS + PRO_JOBS
def job_b(h): return h * B_JOBS + (PRO_JOBS + A_ITERS * A_JOBS)
def job_m(n): return n * M_JOBS + (PRO_JOBS + A_ITERS * A_JOBS + B_HEADS * B_JOBS)
def job_o(n): return n * O_JOBS + (PRO_JOBS + A_ITERS * A_JOBS + B_HEADS * B_JOBS + M_ITERS * M_JOBS)


def fills_a(bank, i): return i
def fills_b(bank, h): return h * (3 if bank < 3 else 2) + fills_a(bank, A_ITERS)
def fills_m(bank, n): return n * 2 + fills_b(bank, B_HEADS)
def fills_o(bank, n): return n + fills_m(bank, M_ITERS)


def ropes_a(i, tile): return i * 2 + (1 + tile)
def ropes_b(h, tile): return h * 6 + (1 + 2 * A_ITERS + tile)


def unit_a(i): return i * A_UNITS
def unit_b(h): return h * B_UNITS + A_ITERS * A_UNITS


def stages(starts, usual, first=None):
    plan = {}
    for k, name in ((0, "normalise"), (2, "values"), (1, "turn_probs"), (3, "scores")):
        for u, start in enumerate(starts):
            late = (first if first and u == 0 else usual) + (0,)
            plan.setdefault(start + late[k], []).append((name, u))
    return plan


A_PLAN = stages([u * 3 for u in range(A_UNITS)], (2, 3, 5), (3, 5, 6))
B_PLAN = stages([1 + u * 5 for u in range(B_UNITS)], (3, 4, 7))
B_PLAN_MERGE = stages([u * 3 for u in range(B_UNITS)], (1, 2, 4))


def groups(spec, together=2):
    job = 0
    for g, (jobs, banks, *tail) in enumerate(spec):
        apart, last_banks = jobs - together, tail[0] if tail else banks
        blocks = [(q, bank, bank == banks[0], bank == banks[-1]) for q in range(apart) for bank in banks]
        blocks += [(q, bank, bank == last_banks[0], bank == last_banks[-1]) for bank in last_banks for q in range(apart, jobs)]
        for n, (q, bank, opens, _) in enumerate(blocks):
            yield job + q, g, q, bank, q == 0, q == jobs - 1, opens, n == 0 or blocks[n - 1][3]
        job += jobs


A_BLOCKS = list(groups([(8, (0, 1, 2, 3))]))
B_BLOCKS = list(groups([(8, (0, 1, 2)), (8, (3, 0, 1, 2), (0, 1, 2, 3)), (8, (0, 1, 2, 3))]))
ROPE_PLAN = {g + 1: (b[1], b[3]) for g, b in enumerate(B_BLOCKS) if b[5] and b[1] < 2 and b[3] < 3}
ROPE_PLAN_FIRST = {g + (2 if b[1] == 0 and b[3] < 2 else 1): (b[1], b[3])
                   for g, b in enumerate(B_BLOCKS) if b[5] and b[1] < 2 and b[3] < 3}
M_BLOCKS = list(groups([(4, (0, 1)), (4, (2, 3)), (2, (0, 1)), (2, (2, 3))], 1))
O_BLOCKS = list(groups([(8, (0, 1, 2, 3))], 1))
O_BLOCKS_LAST = list(groups([(8, (0, 1, 2, 3))], RING))
LN_SPLIT = (1024, 896, 896, 1408)
LN_PARTS = (1, 1, 1, 2)


def build(nc, xT, x, pos, w_in, gate_bias, sinks, w_pa, w_pb, w_out, ln_g, ln_b, rope_rows, mask_a_in, mask_b_in, out):
    with ExitStack() as ctx:
        base = (nc.sbuf_base + 63) // 64 * 64
        fence = ctx.enter_context(nc.sbuf_tensor("arena", [P, (nc.sbuf_usable_end - base - 64) // 4], F32))
        del fence
        top = [base]

        def at(name, offset, shape, dt=F32):
            return nc.alloc_sbuf_tensor_at(name, shape, dt, offset=offset)

        def sb(name, shape, dt=F32):
            n = 4
            for s in shape[1:]:
                n *= s
            where, top[0] = top[0], top[0] + (n + 31) // 32 * 32
            assert top[0] <= nc.sbuf_usable_end
            return at(name, where, shape, dt)

        def sem(name):
            return ctx.enter_context(nc.semaphore(name))

        x_hi, x_lo = sb("x_hi", [P, KT, SEQ], F32R), sb("x_lo", [P, KT, SEQ], F32R)
        raw = sb("raw", [P, RING, SLOT])
        w_hi, w_lo = sb("w_hi", [P, RING, SLOT], F32R), sb("w_lo", [P, RING, SLOT], F32R)
        og_at = top[0]
        og_hi, og_lo = sb("og_hi", [P, 12, SEQ], F32R), sb("og_lo", [P, 12, SEQ], F32R)
        z = at("z", og_at, [P, NR, D])
        g_row, b_row = at("g_row", og_at + 4 * NR * D, [P, D]), at("b_row", og_at + 4 * (NR + 1) * D, [P, D])

        shared_at = top[0]
        q_b, k_b = sb("q_b", [P, B_GROUPS, SEQ]), sb("k_b", [P, B_GROUPS, SEQ])
        branch_at = top[0]
        v_b = sb("v_b", [P, NR, B_GROUPS * B_DH])
        mask_b = sb("mask_b", [P, NR * SEQ + 2 * P])
        probs_b = sb("probs_b", [P, SEQ + 2 * P])
        gate_b = sb("gate_b", [P, SEQ])
        q_a = at("q_a", branch_at, [P, 2, SEQ])
        gate_a = at("gate_a", branch_at + 4096, [P, 2, SEQ])
        v_hi_a, v_lo_a = (at(n, branch_at + where, [P, 4, A_KV, P], F32R)
                          for n, where in (("v_hi_a", 8192), ("v_lo_a", 12288)))
        mask_a = at("mask_a", branch_at + 16384, [P, 2 * P])
        probsT_lo = at("probsT_lo", branch_at + 17408, [P, 4, P], F32R)
        probs_a = at("probs_a", shared_at + 6144, [P, 2, 2, 2 * P + 3])
        q_split = at("q_split", og_at + 8 * 2048, [P, 4, SEQ], F32R)
        k_hi_a, k_lo_a = (at(n, og_at + 4 * 12 * SEQ + 8 * 2048 + where, [P, A_KV, SEQ], F32R)
                          for n, where in (("k_hi_a", 0), ("k_lo_a", 4096)))
        angle, turns = (at(n, shared_at + 2048 * k, [P, SEQ]) for k, n in enumerate(("angle", "turns")))
        rests = [at(f"rest{k}", where, [P, SEQ]) for k, where in
                 enumerate((shared_at + 2 * 2048, branch_at + 2048, branch_at + 4096, branch_at + 6144))]
        pos_row = at("pos_row", shared_at + 3 * 2048, [P, SEQ], I32)
        k_rot = at("k_rot", shared_at + 4 * 2048, [P, SEQ])
        vT_a = at("vT_a", shared_at + 5 * 2048, [P, SEQ])
        merged = at("merged", shared_at, [P, KT, SEQ])

        probsT_at = top[0]
        probsT = sb("probsT", [P, 6, P])
        probsT_hi = at("probsT_hi", probsT_at, [P, 4, P], F32R)
        shifted = sb("shifted", [P, SEQ])
        tables_at = top[0]
        cos_a, sin_a, cos_b, sin_b = (sb(n, [P, SEQ]) for n in ("cos_a", "sin_a", "cos_b", "sin_b"))
        part_a, part_b = at("part_a", tables_at, [P, 2, SEQ]), at("part_b", tables_at + 4096, [P, 2, SEQ])
        ident = sb("ident", [P, P])
        rope_col = sb("rope_col", [P, 4])
        gbias = sb("gbias", [P, 2 * KT])
        sink_row = sb("sink_row", [P, A_HEADS])
        sink_pair = sb("sink_pair", [P, A_HEADS, 2])
        rowmax, negmax = sb("rowmax", [P, 2, 2]), sb("negmax", [P, 2, 2])
        denom, rdenom = sb("denom", [P, 2, 2]), sb("rdenom", [P, 2, 2])
        stats = sb("stats", [P, NR, O_ITERS, 6])
        variance, root, correction = sb("variance", [P, NR]), sb("root", [P, NR]), sb("correction", [P, NR])
        meanvar, rstd, shift = sb("meanvar", [P, NR, 2]), sb("rstd", [P, NR]), sb("shift", [P, NR])

        acc = [ctx.enter_context(nc.psum_tensor(f"acc{b}", [P, SEQ], F32)) for b in range(4)]
        ps_scores = ctx.enter_context(nc.psum_tensor("ps_scores", [P, 2 * SEQ], F32))
        ps_turn = ctx.enter_context(nc.psum_tensor("ps_turn", [P, SEQ], F32))
        ps_out = ctx.enter_context(nc.psum_tensor("ps_out", [P, SEQ], F32))

        raw_in = [sem(f"raw_in{s}") for s in range(RING)]
        x_lo_done, kv_full, k_read = sem("x_lo_done"), sem("kv_full"), sem("k_read")
        hi_done, lo_done, slot_used = sem("hi_done"), sem("lo_done"), sem("slot_used")
        full, free = [sem(f"full{b}") for b in range(4)], [sem(f"free{b}") for b in range(4)]
        small_in, mask_b_in_sem, row_in, store = sem("small_in"), sem("mask_b_loaded"), sem("row_in"), sem("store")
        x_in = [sem(f"x_in{r}") for r in range(NR)]
        pos_in = sem("pos_in")
        ident_step, table_step, table_arg, table_done = sem("ident_step"), sem("table_step"), sem("table_arg"), sem("table_done")
        sink_step, sink_set = sem("sink_step"), sem("sink_set")
        swapped, rope_parts, rope_done = sem("swapped"), sem("rope_parts"), sem("rope_done")
        v_out, v_turned, v_hi_ready, v_a_ready = sem("v_out"), sem("v_turned"), sem("v_hi_ready"), sem("v_a_ready")
        k_split, q_hi_done, q_ready = sem("k_split"), sem("q_hi_done"), sem("q_ready")
        sig_ready = sem("sig_ready")
        masked_ready = sem("masked_ready")
        scores_ready, rowmax_ready, negmax_ready = sem("scores_ready"), sem("rowmax_ready"), sem("negmax_ready")
        probs_ready, probsT_psum, probsT_ready = sem("probs_ready"), sem("probsT_psum"), sem("probsT_ready")
        probsT_rest, recip_ready, normalised = sem("probsT_rest"), sem("recip_ready"), sem("normalised")
        out_psum, out_gated = sem("out_psum"), sem("out_gated")
        og_hi_ready, og_ready = sem("og_hi_ready"), sem("og_ready")
        merge_sig, merged_ready = sem("merge_sig"), sem("merged_ready")
        merged_hi_ready, merged_lo_ready = sem("merged_hi_ready"), sem("merged_lo_ready")
        var_ready, root_ready = sem("var_ready"), sem("root_ready")
        stats_ready, ln_step, centred, scaled, finished = (sem("stats_ready"), sem("ln_step"), sem("centred"),
                                                           sem("scaled"), sem("finished"))

        w_in_v = w_in.rearrange("(k p) c -> p k c", p=P)
        w_pa_v = w_pa.rearrange("(k p) c -> p k c", p=P)
        w_pb_v = w_pb.rearrange("(k p) c -> p k c", p=P)
        w_out_v = w_out.rearrange("(k p) c -> p k c", p=P)
        xT_v = xT.rearrange("(k p) s -> p k s", p=P)
        x_v = x.rearrange("(j r) d -> r j d", r=NR)
        out_v = out.rearrange("b (j r) d -> r (b j) d", r=NR)

        def by_block(t):
            return t.rearrange("p (b r j) -> p r b j", b=4, r=NR)

        def by_residue(t):
            return t.rearrange("p (r b j) -> p r b j", b=4, r=NR)

        def twice(t):
            return t.rearrange("p b v (c d) -> p (b v) c d", c=2)

        def turned_v():
            return ps_turn.rearrange("p (n d) -> p n d", d=A_DH).unsqueeze(2).to_broadcast([P, 8, 2, A_DH])

        def swap_place(first, group, tile):
            return q_a[:, tile - 1, :] if first and group == 0 and tile > 0 else shifted[:]

        block = ctx.enter_context(nc.Block())

        @block.sync
        def _(sp):
            def job(n, first, off, pieces):
                slot = off % RING
                loads = reversed(list(pieces(raw[:, slot, :])))
                if not first:
                    sp.wait_ge(lo_done, n + (off - RING + 1 - PRO_JOBS + 4))
                for dst, src in loads:
                    sp.dma_start(dst, src).then_inc(raw_in[slot], 16)

            def wait_split(n):
                m, part = divmod(n, 3)
                if part == 0:
                    sp.wait_ge(lo_done, m + 1)
                else:
                    sp.wait_ge(x_lo_done, 2 * m + part)

            def halves(dst, src):
                return [(dst[h:h + P // 2], src[h:h + P // 2]) for h in (0, P // 2)]

            def load_a(i, q):
                def pieces(t):
                    for half, col in enumerate((QA, GA)):
                        for k in range(2):
                            c = 512 * half + 256 * k
                            src = w_in_v[:, 2 * q + k, col:col + A_WIDTH].rearrange("p (v c) -> p v c", v=A_KV)
                            yield (t[:, c:c + 256].rearrange("p (v c) -> p v c", v=A_KV), src[:, :, bass.ds(i * P, P)])
                return pieces

            def load_b(h, g, q):
                def pieces(t):
                    col = (QB, KB, VB)[g]
                    for k in range(2):
                        c = (512 if g == 1 else 384) * k
                        src = w_in_v[:, 2 * q + k, col:col + B_GROUPS * GW].rearrange("p (g c) -> p g c", g=B_GROUPS)
                        dst = t[:, c:c + 384].rearrange("p (g c) -> p g c", g=B_GROUPS)
                        if g == 1:
                            yield dst, src[:, :, bass.ds(h * P, P)]
                            yield t[:, c + 384:c + 512], w_in_v[:, 2 * q + k, GB:GB + GW][:, bass.ds(h * P, P)]
                        else:
                            yield from halves(dst, src[:, :, bass.ds(h * P, P)])
                return pieces

            def load_m(n, g, q):
                def pieces(t):
                    cols = bass.ds(n * 256, 256)
                    for k in range(4):
                        if g < 2:
                            yield (t[:, 256 * k:256 * k + 256],
                                   w_in_v[:, 4 * q + k, MG + D * g:MG + D * (g + 1)][:, cols])
                        elif g == 2:
                            yield t[:, 256 * k:256 * k + 256], w_pa_v[:, 4 * q + k, cols]
                        elif k < 2:
                            yield from halves(t[:, 256 * k:256 * k + 256], w_pb_v[:, 2 * q + k, cols])
                return pieces

            def load_o(n, q):
                return lambda t: [part for k in range(2)
                                  for part in halves(t[:, 512 * k:512 * k + 512], w_out_v[:, 2 * q + k, bass.ds(n * 512, 512)])]

            for n in range(PRO_JOBS):
                m, part = divmod(n, 3)
                slot = n % RING
                if n >= RING:
                    wait_split(n - RING)
                if part == 0:
                    sp.dma_start(raw[:, slot, :].rearrange("p (k c) -> p k c", k=4), w_in_v[:, 4 * m:4 * m + 4, KA:GA])\
                        .then_inc(raw_in[slot], 16)
                else:
                    k = 4 * m + 2 * (part - 1)
                    sp.dma_start(raw[:, slot, :].rearrange("p (k c) -> p k c", k=2), xT_v[:, k:k + 2, :])\
                        .then_inc(raw_in[slot], 16)
                if n == 2:
                    sp.dma_start(rope_col[:], rope_rows).then_inc(pos_in, 16)
                    sp.dma_start(pos_row[:], pos.partition_broadcast(P)).then_inc(pos_in, 16)
            for q in range(RING):
                wait_split(PRO_JOBS - RING + q)
                job(None, True, q, load_a(0, q))
            sp.dma_start(mask_a[:], mask_a_in).then_inc(small_in, 16)
            sp.dma_start(sink_row[:], sinks.partition_broadcast(P)).then_inc(small_in, 16)
            sp.dma_start(gbias[:], gate_bias).then_inc(small_in, 16)

            def iter_a(i, done):
                for q in range(done, A_JOBS):
                    job(job_a(i), False, q, load_a(i, q))

            def iter_b(h, first):
                for k in range(B_JOBS):
                    job(job_b(h), False, k, load_b(h, k // 8, k % 8))
                    if first and k == 15:
                        sp.wait_ge(og_ready, 2 * A_ITERS)
                        sp.dma_start(mask_b[:], mask_b_in).then_inc(mask_b_in_sem, 16)

            def iter_m(n):
                for k in range(M_JOBS):
                    g, q = ((0, k) if k < 4 else (1, k - 4) if k < 8 else (2, k - 8) if k < 10 else (3, k - 10))
                    job(job_m(n), False, k, load_m(n, g, q))

            def iter_o(n, first):
                for q in range(O_JOBS):
                    job(job_o(n), False, q, load_o(n, q))
                    if first and q == 4:
                        sp.wait_ge(full[3], fills_m(3, M_ITERS))
                    if first and q >= 4:
                        sp.dma_start(z[:, q - 4, :], x_v[q - 4]).then_inc(x_in[q - 4], 16)
                if first:
                    sp.dma_start(g_row[:], ln_g.partition_broadcast(P)).then_inc(row_in, 16)
                    sp.dma_start(b_row[:], ln_b.partition_broadcast(P)).then_inc(row_in, 16)

            iter_a(0, RING)
            with sp.Fori(1, A_ITERS) as i:
                iter_a(i, 0)
            iter_b(0, True)
            with sp.Fori(1, B_HEADS) as h:
                iter_b(h, False)
            with sp.Fori(0, M_ITERS) as n:
                iter_m(n)
            iter_o(0, True)
            with sp.Fori(1, O_ITERS) as n:
                iter_o(n, False)
            for r in range(NR):
                width = LN_SPLIT[r] // LN_PARTS[r]
                for part in range(LN_PARTS[r]):
                    columns = slice(width * part, width * (part + 1))
                    sp.wait_ge(scaled, 2 * (r + part) + 2)
                    sp.dma_start(out_v[r, :, columns], z[:, r, columns]).then_inc(store, 16)
                sp.wait_ge(finished, 2 * r + 2)
                sp.dma_start(out_v[r, :, LN_SPLIT[r]:D], z[:, r, LN_SPLIT[r]:D]).then_inc(store, 16)
            sp.wait_ge(store, 16 * (NR + sum(LN_PARTS)))

        @block.gpsimd
        def _(pool):
            nc.gpsimd.memset(ident[:], 0.0).then_inc(ident_step, 1)
            pool.wait_ge(ident_step, 1)
            nc.gpsimd.affine_select(out=ident[:], in_=ident[:], compare_op=ALU.not_equal, fill=1.0, base=0,
                                    pattern=[[-1, P]], channel_multiplier=1).then_inc(ident_step, 1)

            def low(dst, slot, hi, n):
                pool.wait_ge(hi_done, n + 1)
                nc.gpsimd.tensor_tensor(dst, raw[:, slot, :], hi.bitcast(F32), ALU.subtract).then_inc(lo_done, 1)

            for m in range(4):
                low(w_lo[:, m, :], 3 * m % RING, w_hi[:, m, :], 3 * m)
            with pool.Fori(0, (job_o(O_ITERS) - PRO_JOBS) // RING) as i:
                for s in range(RING):
                    low(w_lo[:, s, :], s, w_hi[:, s, :], i * RING + (PRO_JOBS + s))
            pool.wait_ge(row_in, 32)
            for r in range(NR):
                columns = z[:, r, LN_SPLIT[r]:D]
                pool.wait_ge(centred, r + 1)
                nc.gpsimd.tensor_tensor(columns, columns, g_row[:, LN_SPLIT[r]:D], ALU.mult).then_inc(finished, 1)
                pool.wait_ge(finished, 2 * r + 1)
                nc.gpsimd.tensor_tensor(columns, columns, b_row[:, LN_SPLIT[r]:D], ALU.add).then_inc(finished, 1)

        @block.scalar
        def _(act):
            def high(n, off):
                s = off % RING
                act.wait_ge(raw_in[s], n * (16 * LOADS // RING) +
                            (16 * LOADS * (off // RING + 1) - 16 * (LOADS - 1) * PRO_JOBS // RING))
                act.wait_ge(slot_used, n + (off - 2 * RING - RING + 1))
                nc.scalar.activation(w_hi[:, s, :], raw[:, s, :], ACT.Copy).then_inc(hi_done, 1)

            def exps_a(u, a):
                b, j = divmod(u, 2)
                lo = P if b == 0 else 0
                act.wait_ge(negmax_ready, a + 1)
                for hh in range(2):
                    s = probs_a[:, j, hh, lo:2 * P + 1]
                    e = nc.scalar.activation(s, s, ACT.Exp, bias=negmax[:, j, hh:hh + 1], scale=A_SCALE,
                                             accum_out=denom[:, j, hh:hh + 1])
                e.then_inc(probs_ready, 1)

            def exps_b(u, a):
                act.wait_ge(negmax_ready, a + 1)
                nc.scalar.activation(probs_b[:], probs_b[:], ACT.Exp, bias=negmax[:, u % 2, 0:1], scale=B_SCALE,
                                     accum_out=denom[:, u % 2, 0:1]).then_inc(probs_ready, 1)

            def probs_out(kind, u, a):
                act.wait_ge(probsT_psum, a + 1)
                if kind == "b" or u:
                    act.wait_ge(out_psum, a)
                c = 2 if kind == "a" and u < 2 else 0
                dst = (probsT_hi if kind == "a" else probsT)[:, c:4, :]
                src = ps_turn[:, c * P:4 * P].rearrange("p (c q) -> p c q", q=P)
                nc.scalar.activation(dst, src, ACT.Copy).then_inc(probsT_ready, 1)

            def q_high(i):
                act.wait_ge(rope_done, ropes_a(i, 2))
                for hh in range(2):
                    rows = slice(A_DH * hh, A_DH * hh + A_DH)
                    nc.scalar.activation(q_split[rows, 2 + hh, :], q_a[rows, 1, :], ACT.Copy).then_inc(q_hi_done, 1)

            def attend(kind, plan, g, first_unit, i):
                if kind == "a" and g == 0:
                    q_high(i)
                for stage, u in plan.get(g, ()):
                    if stage == "scores":
                        (exps_a if kind == "a" else exps_b)(u, first_unit + u)
                    if stage == "turn_probs":
                        probs_out(kind, u, first_unit + u)

            for n in range(PRO_JOBS):
                m, part = divmod(n, 3)
                act.wait_ge(raw_in[n % RING], 16 * (n // RING + 1))
                k = 4 * m + 2 * (part - 1)
                dst = w_hi[:, m, :] if part == 0 else x_hi[:, k:k + 2, :].rearrange("p k c -> p (k c)")
                nc.scalar.activation(dst, raw[:, n % RING, :], ACT.Copy).then_inc(hi_done, 1)
            for off in range(AHEAD):
                high(job_a(0), off)

            def swap_halves(dst, src, half, done):
                if not (isinstance(done, int) and done == 0):
                    act.wait_ge(rope_done, done)
                for k in range(P // half):
                    last = nc.scalar.activation(dst[half * k:half * (k + 1), :],
                                                src[half * (k ^ 1):half * ((k ^ 1) + 1), :], ACT.Copy)
                last.then_inc(swapped, 1)

            def sines(k):
                table, col = ((cos_a, None), (sin_a, 3), (cos_b, None), (sin_b, 1))[k]
                act.wait_ge(table_arg, k + 1)
                scale = 1.0 if col is None else rope_col[:, col:col + 1]
                nc.scalar.activation(table[:], rests[k][:], ACT.Sin, scale=scale).then_inc(table_done, 1)

            def iter_a(i, with_attention):
                for g, (job, _, _, bank, _, last, opens, _) in enumerate(A_BLOCKS):
                    if with_attention:
                        attend("a", A_PLAN, g, unit_a(i - 1), i - 1)
                    if not with_attention and g == 2:
                        act.wait_ge(kv_full, 2)
                        nc.scalar.activation(by_block(vT_a[:]), by_residue(ps_out[:]), ACT.Copy).then_inc(v_out, 1)
                        swap_halves(shifted[:], ps_scores[:, 0:SEQ], 32, 0)
                    if not with_attention and g in (13, 21):
                        for k in (0, 1) if g == 13 else (2, 3):
                            sines(k)
                    if not with_attention and g == 10:
                        act.wait_ge(v_turned, 1)
                        nc.scalar.activation(twice(v_hi_a), turned_v(), ACT.Copy).then_inc(v_hi_ready, 1)
                    if last and bank < 2:
                        act.wait_ge(full[bank], fills_a(bank, i) + 1)
                        swap_halves(shifted[:], acc[bank][:], 32, ropes_a(i, bank))
                    if last and bank >= 2:
                        act.wait_ge(full[bank], fills_a(bank, i) + 1)
                        if not with_attention and bank == 2:
                            act.wait_ge(table_done, 4)
                        if with_attention and bank == 2:
                            act.wait_ge(og_ready, i * 2)
                        nc.scalar.activation(by_block(gate_a[:, bank - 2, :]), by_residue(acc[bank][:]), ACT.Sigmoid)\
                            .then_inc(sig_ready, 1)
                    if opens:
                        high(job_a(i), job + AHEAD)

            def iter_b(h, first):
                for g, (job, group, _, bank, _, last, opens, _) in enumerate(B_BLOCKS):
                    if first:
                        attend("a", A_PLAN, g, unit_a(A_ITERS - 1), A_ITERS - 1)
                    else:
                        attend("b", B_PLAN, g, unit_b(h - 1), h - 1)
                    if last and group < 2 and bank < 3:
                        act.wait_ge(full[bank], fills_b(bank, h) + (group + 1))
                        if first and group == 0 and bank > 0:
                            act.wait_ge(q_ready, 4 * A_ITERS)
                            swap_halves(swap_place(first, group, bank), acc[bank][:], 64, 0)
                        else:
                            swap_halves(shifted[:], acc[bank][:], 64, ropes_b(h, 3 * group + bank))
                    if last and group == 1 and bank == 3:
                        act.wait_ge(full[3], fills_b(3, h) + 1)
                        act.wait_ge(og_ready, h + 2 * A_ITERS)
                        nc.scalar.activation(gate_b[:], acc[3][:], ACT.Sigmoid).then_inc(sig_ready, 1)
                    if last and group == 2:
                        act.wait_ge(full[bank], fills_b(bank, h) + (3 if bank < 3 else 2))
                        act.wait_ge(out_psum, unit_b(h))
                        nc.scalar.activation(v_b[:, bank, :], acc[bank][:, 0:384], ACT.Copy).then_inc(free[bank], 1)
                    if opens:
                        high(job_b(h), job + AHEAD)

            def iter_m(n, first, last_iter):
                for g, (job, group, _, bank, _, last, opens, _) in enumerate(M_BLOCKS):
                    if opens:
                        high(job_m(n), job + AHEAD)
                    if first:
                        attend("b", B_PLAN_MERGE, g, unit_b(B_HEADS - 1), B_HEADS - 1)
                    if last and group < 2:
                        act.wait_ge(full[bank], fills_m(bank, n) + 1)
                        if not first and bank % 2 == 0:
                            act.wait_ge(merged_ready, n * 2)
                        part, t = (part_a, part_b)[group], bank % 2
                        nc.scalar.activation(part[:, t, :], acc[bank][:], ACT.Sigmoid,
                                             bias=gbias[:, bass.ds(n * 2 + (KT * group + t), 1)]).then_inc(merge_sig, 1)
                    if last_iter and group == 2 and job == 8 and bank == 1:
                        merged_high(0, 4, 12)
                        merged_high(4, 8, 12)
                    if last_iter and group == 2 and job == 9 and bank == 1:
                        merged_high(8, 12, 12)
                        merged_high(12, 14, 14)

            def merged_high(lo, hi, ready):
                act.wait_ge(merged_ready, ready)
                act.wait_ge(full[3], fills_m(3, M_ITERS - 1) + 1)
                nc.scalar.activation(x_hi[:, lo:hi, :], merged[:, lo:hi, :], ACT.Copy).then_inc(merged_hi_ready, 1)

            def iter_o(n, last_iter):
                for g, (job, _, _, bank, _, last, opens, _) in enumerate(O_BLOCKS):
                    if opens and not (last_iter and job + AHEAD >= O_JOBS):
                        high(job_o(n), job + AHEAD)

            iter_a(0, False)
            with act.Fori(1, A_ITERS) as i:
                iter_a(i, True)
            iter_b(0, True)
            with act.Fori(1, B_HEADS) as h:
                iter_b(h, False)
            iter_m(0, True, False)
            with act.Fori(1, M_ITERS - 1) as n:
                iter_m(n, False, False)
            iter_m(M_ITERS - 1, False, True)
            merged_high(14, 16, 16)
            with act.Fori(0, O_ITERS - 1) as n:
                iter_o(n, False)
            iter_o(O_ITERS - 1, True)
            for r in range(NR):
                act.wait_ge(var_ready, r + 1)
                nc.scalar.activation(root[:, r:r + 1], variance[:, r:r + 1], ACT.Sqrt).then_inc(root_ready, 1)
                act.wait_ge(ln_step, 6 * r + 6)
                columns = z[:, r, LN_SPLIT[r]:D]
                nc.scalar.activation(columns, columns, ACT.Identity, bias=shift[:, r:r + 1],
                                     scale=rstd[:, r:r + 1]).then_inc(centred, 1)

        @block.vector
        def _(dve):
            step = [0]

            def chain(instruction):
                step[0] += 1
                instruction.then_inc(table_step, 1)
                dve.wait_ge(table_step, step[0])

            two_pi = 6.283185307179586
            c1 = 6.28125
            c2 = 0.0019350051879882812
            c3 = two_pi - c1 - c2
            magic = 1.5 * 2.0 ** 23
            pi = 3.141592

            def reduce_angle(dst, src, unit, offset):
                chain(nc.vector.tensor_scalar(turns[:], src, 1.0 / (two_pi * unit), offset, ALU.mult, ALU.add))
                chain(nc.vector.tensor_scalar(turns[:], turns[:], magic, -magic, ALU.add, ALU.add))
                for k, c in enumerate((c1, c2, c3)):
                    chain(nc.vector.scalar_tensor_tensor(dst, turns[:], -c * unit, src if k == 0 else dst,
                                                         ALU.mult, ALU.add))

            def x_low(e):
                n = 3 * (e // 2) + 1 + e % 2
                dve.wait_ge(hi_done, n + 1)
                lo, hi = (t[:, 2 * e:2 * e + 2, :].rearrange("p k c -> p (k c)") for t in (x_lo, x_hi))
                nc.vector.tensor_tensor(lo, raw[:, n % RING, :], hi.bitcast(F32), ALU.subtract).then_inc(x_lo_done, 1)

            for e in range(8):
                x_low(e)
            dve.wait_ge(pos_in, 32)
            for k, (freq, quarter) in enumerate(((2, True), (2, False), (0, True), (0, False))):
                rest = rests[k]
                if quarter:
                    chain(nc.vector.tensor_copy(angle[:], pos_row[:]))
                    chain(nc.vector.tensor_scalar(angle[:], angle[:], rope_col[:, freq:freq + 1], None, ALU.mult))
                    reduce_angle(angle[:], angle[:], 65536.0, 0.0)
                reduce_angle(rest[:], angle[:], 1.0, 0.25 if quarter else 0.0)
                chain(nc.vector.tensor_scalar(rest[:], rest[:], two_pi / 4 if quarter else 0.0, -pi, ALU.add, ALU.max))
                nc.vector.tensor_scalar(rest[:], rest[:], pi, None, ALU.min).then_inc(table_arg, 1)
            dve.wait_ge(small_in, 48)
            nc.vector.tensor_scalar(sink_pair[:, :, 0], sink_row[:], 1.0 / A_SCALE, None, ALU.mult).then_inc(sink_step, 1)
            nc.vector.tensor_scalar(sink_pair[:, :, 1], sink_row[:], -1.0, None, ALU.mult).then_inc(sink_step, 1)
            dve.wait_ge(sink_step, 2)
            dve.wait_ge(table_done, 2)

            def rope(dst, swapped_src, src, src_full, src_free, filled, done, branch, cos, sin):
                to_order, from_order = (by_block, by_residue) if branch == "a" else (lambda t: t, lambda t: t)
                dve.wait_ge(src_full, filled)
                dve.wait_ge(swapped, done + 1)
                nc.vector.tensor_tensor(to_order(dst), from_order(src), from_order(cos[:]), ALU.mult).then_inc(rope_parts, 1)
                nc.vector.tensor_tensor(swapped_src, swapped_src, sin[:], ALU.mult).then_inc(src_free, 1)
                dve.wait_ge(rope_parts, done + 1)
                dve.wait_ge(src_free, filled)
                nc.vector.tensor_tensor(to_order(dst), to_order(dst), from_order(swapped_src), ALU.add).then_inc(rope_done, 1)

            def mask_max_a(u, a):
                b, j = divmod(u, 2)
                lo = P if b == 0 else 0
                dve.wait_ge(scores_ready, a + 1)
                if u >= 2:
                    dve.wait_ge(probsT_psum, a - 1)
                nc.vector.tensor_copy(probs_a[:, j, :, 2 * P:2 * P + 1], probs_a[:, j, :, 2 * P + 1:2 * P + 2])
                masked = probs_a[:, j, :, lo:2 * P]
                nc.vector.tensor_tensor(masked, ps_scores[:].rearrange("p (h k) -> p h k", h=2)[:, :, lo:2 * P],
                                        mask_a[:, lo:2 * P].unsqueeze(1).to_broadcast([P, 2, 2 * P - lo]), ALU.add)\
                    .then_inc(masked_ready, 1)
                dve.wait_ge(masked_ready, a + 1)
                nc.vector.tensor_reduce(rowmax[:, j, :], masked, mybir.AxisListType.X, ALU.max).then_inc(rowmax_ready, 1)
                dve.wait_ge(rowmax_ready, a + 1)
                nc.vector.scalar_tensor_tensor(negmax[:, j, :], rowmax[:, j, :], -A_SCALE, probs_a[:, j, :, 2 * P + 2],
                                               ALU.mult, ALU.min).then_inc(negmax_ready, 1)

            def mask_max_b(u, a):
                dve.wait_ge(scores_ready, a + 1)
                dve.wait_ge(probsT_psum, a)
                nc.vector.tensor_tensor(probs_b[:, 0:SEQ], ps_scores[:, 0:SEQ], mask_b[:, u * SEQ:(u + 1) * SEQ], ALU.add)
                nc.vector.tensor_tensor(probs_b[:, SEQ:SEQ + 2 * P], ps_scores[:, SEQ:SEQ + 2 * P],
                                        mask_b[:, NR * SEQ:NR * SEQ + 2 * P], ALU.add).then_inc(masked_ready, 1)
                dve.wait_ge(masked_ready, a + 1)
                nc.vector.tensor_reduce(rowmax[:, u % 2, 0:1], probs_b[:], mybir.AxisListType.X, ALU.max)\
                    .then_inc(rowmax_ready, 1)
                dve.wait_ge(rowmax_ready, a + 1)
                nc.vector.tensor_scalar(negmax[:, u % 2, 0:1], rowmax[:, u % 2, 0:1], -B_SCALE, None, ALU.mult)\
                    .then_inc(negmax_ready, 1)

            def normalise(kind, u, a):
                j = u % 2
                dve.wait_ge(probs_ready, a + 1)
                n = 2 if kind == "a" else 1
                nc.vector.reciprocal(rdenom[:, j, 0:n], denom[:, j, 0:n]).then_inc(recip_ready, 1)
                dve.wait_ge(recip_ready, a + 1)
                for hh in range(n):
                    p = probs_a[:, j, hh, (P if u < 2 else 0):2 * P] if kind == "a" else probs_b[:]
                    last = nc.vector.tensor_scalar(p, p, rdenom[:, j, hh:hh + 1], None, ALU.mult)
                last.then_inc(normalised, 1)

            def probs_rest(kind, u, a):
                if kind == "a":
                    c = 2 if u < 2 else 0
                    dve.wait_ge(probsT_ready, a + 1)
                    if u:
                        dve.wait_ge(out_psum, a)
                    nc.vector.tensor_tensor(probsT_lo[:, c:4, :], ps_turn[:, c * P:4 * P].rearrange("p (c q) -> p c q", q=P),
                                            probsT_hi[:, c:4, :].bitcast(F32), ALU.subtract).then_inc(probsT_rest, 1)
                else:
                    dve.wait_ge(probsT_psum, a + 1)
                    dve.wait_ge(out_psum, a)
                    nc.vector.tensor_copy(probsT[:, 4:6, :],
                                          ps_scores[:, SEQ + 2 * P:2 * SEQ].rearrange("p (c q) -> p c q", c=2))\
                        .then_inc(probsT_rest, 1)

            def split_gated(kind, gated, tile, done):
                hi, lo = (t[:, bass.ds(tile, 1), :].rearrange("p t s -> p (t s)") for t in (og_hi, og_lo))
                if kind == "a":
                    hi, lo, gated = by_residue(hi), by_residue(lo), by_block(gated)
                nc.vector.tensor_copy(hi, gated).then_inc(og_hi_ready, 1)
                dve.wait_ge(og_hi_ready, done + 1)
                nc.vector.tensor_tensor(lo, gated, hi.bitcast(F32), ALU.subtract).then_inc(og_ready, 1)

            def gate_out(kind, u, a, i, late):
                dve.wait_ge(out_psum, a + 1)
                b, j = divmod(u, 2)
                if kind == "a":
                    for hh in range(2):
                        g = gate_a[half[hh], j, b * P:(b + 1) * P]
                        last = nc.vector.tensor_tensor(g, ps_out[half[hh], hh * P:hh * P + P], g, ALU.mult)
                else:
                    g = gate_b[:, u * P:(u + 1) * P]
                    last = nc.vector.tensor_tensor(g, ps_out[:, 0:P], g, ALU.mult)
                last.then_inc(out_gated, 1)
                if kind == "a" and b == 3 and (j or not late):
                    dve.wait_ge(out_gated, a + 1)
                    for tile in (0, 1) if late else (j,):
                        split_gated(kind, gate_a[:, tile, :], i + A_ITERS * tile, i * 2 + tile)
                if kind == "b" and u == 3:
                    dve.wait_ge(out_gated, a + 1)
                    split_gated(kind, gate_b[:], i + 2 * A_ITERS, i + 2 * A_ITERS)

            def attend(kind, plan, g, first_unit, i, late=False):
                if kind == "a" and g == 0:
                    nc.vector.tensor_copy(probs_a[:, :, :, 2 * P + 1:2 * P + 3].rearrange("p j v c -> p (j v) c"),
                                          sink_pair[:, bass.ds(i * 4, 4), :]).then_inc(sink_set, 1)
                    dve.wait_ge(sink_set, i + 1)
                    split_q(1, i * 2)
                if kind == "b" and g == 0:
                    dve.wait_ge(mask_b_in_sem, 16)
                for stage, u in plan.get(g, ()):
                    a = first_unit + u
                    if stage == "scores":
                        (mask_max_a if kind == "a" else mask_max_b)(u, a)
                    elif stage == "normalise":
                        normalise(kind, u, a)
                    elif stage == "turn_probs":
                        probs_rest(kind, u, a)
                    elif stage == "values":
                        gate_out(kind, u, a, i, late)

            def gate(dst, src, bank, done):
                dve.wait_ge(sig_ready, done + 1)
                nc.vector.tensor_tensor(dst, src, dst, ALU.mult).then_inc(free[bank], 1)

            dve.wait_ge(v_hi_ready, 1)
            nc.vector.tensor_tensor(twice(v_lo_a), turned_v(), twice(v_hi_a).bitcast(F32), ALU.subtract).then_inc(v_a_ready, 1)
            rope(k_rot[:], shifted[:], ps_scores[:, 0:SEQ], kv_full, k_read, 1, 0, "a", cos_a, sin_a)
            dve.wait_ge(rope_done, 1)
            half = [slice(A_DH * hh, A_DH * hh + A_DH) for hh in range(2)]
            for kv in range(A_KV):
                for hh in range(2):
                    nc.vector.tensor_copy(k_hi_a[half[hh], kv, :], k_rot[half[kv], :]).then_inc(k_split, 1)
            dve.wait_ge(k_split, 4)
            for kv in range(A_KV):
                for hh in range(2):
                    nc.vector.tensor_tensor(k_lo_a[half[hh], kv, :], k_rot[half[kv], :],
                                            k_hi_a[half[kv], kv, :].bitcast(F32), ALU.subtract).then_inc(k_split, 1)

            def split_q(j, done):
                dve.wait_ge(rope_done, done + 2 + j)
                if j == 0:
                    for hh in range(2):
                        nc.vector.tensor_copy(q_split[half[hh], hh, :], q_a[half[hh], 0, :]).then_inc(q_hi_done, 1)
                dve.wait_ge(q_hi_done, done * 2 + (2 * j + 2))
                for hh in range(2):
                    nc.vector.tensor_tensor(q_split[half[1 - hh], 2 * j + hh, :], q_a[half[hh], j, :],
                                            q_split[half[hh], 2 * j + hh, :].bitcast(F32), ALU.subtract).then_inc(q_ready, 1)

            def iter_a(i, with_attention):
                for g, (job, _, _, bank, _, last, opens, _) in enumerate(A_BLOCKS):
                    if with_attention:
                        attend("a", A_PLAN, g, unit_a(i - 1), i - 1)
                    if A_BLOCKS[g - 1][2:4] == (A_JOBS - 1, 0):
                        rope_q(i, 0)
                        if with_attention:
                            dve.wait_ge(scores_ready, unit_a(i))
                        split_q(0, i * 2)
                    if A_BLOCKS[g - 1][2:4] == (A_JOBS - 1, 1):
                        rope_q(i, 1)
                    if last and bank >= 2:
                        gate(by_block(gate_a[:, bank - 2, :]), by_residue(acc[bank][:]), bank, i * 2 + (bank - 2))

            def rope_q(i, j):
                rope(q_a[:, j, :], shifted[:], acc[j][:], full[j], free[j], fills_a(j, i) + 1, ropes_a(i, j), "a", cos_a, sin_a)

            def iter_b(h, first):
                for g, (job, group, _, bank, _, last, opens, _) in enumerate(B_BLOCKS):
                    if first:
                        attend("a", A_PLAN, g, unit_a(A_ITERS - 1), A_ITERS - 1, late=True)
                    else:
                        attend("b", B_PLAN, g, unit_b(h - 1), h - 1)
                    done_group, tile = ROPE_PLAN_FIRST.get(g, (2, 0)) if first else ROPE_PLAN.get(g, (2, 0))
                    if done_group < 2:
                        if not first and done_group == 0 and tile == 0:
                            dve.wait_ge(scores_ready, unit_b(h))
                        rope((q_b, k_b)[done_group][:, tile, :], swap_place(first, done_group, tile), acc[tile][:],
                             full[tile], free[tile], fills_b(tile, h) + (done_group + 1), ropes_b(h, 3 * done_group + tile), "b", cos_b, sin_b)
                    if last and group == 1 and bank == 3:
                        gate(gate_b[:], acc[3][:], 3, h + 2 * A_ITERS)

            def iter_m(n, first):
                for g, (job, group, _, bank, _, last, opens, _) in enumerate(M_BLOCKS):
                    if first:
                        attend("b", B_PLAN_MERGE, g, unit_b(B_HEADS - 1), B_HEADS - 1)
                    if last and group < 2:
                        dve.wait_ge(merge_sig, n * 4 + (2 * group + bank % 2 + 1))
                        dve.sem_inc(free[bank], 1)
                    if last and group >= 2:
                        t = bank % 2
                        part = (part_a, part_b)[group - 2]
                        dve.wait_ge(full[bank], fills_m(bank, n) + 2)
                        nc.vector.tensor_tensor(part[:, t, :], acc[bank][:], part[:, t, :], ALU.mult)\
                            .then_inc(free[bank], 1)
                        if group == 3:
                            dve.wait_ge(free[bank], fills_m(bank, n) + 2)
                            dve.wait_ge(free[t], fills_m(t, n) + 2)
                            nc.vector.tensor_tensor(merged[:, bass.ds(n * 2 + t, 1), :].rearrange("p k c -> p (k c)"),
                                                    part_a[:, t, :], part_b[:, t, :], ALU.add).then_inc(merged_ready, 1)
                    if isinstance(n, int) and n == M_ITERS - 1 and (job, bank) == (8, 1):
                        merged_low(0, 4, 1)
                        merged_low(4, 8, 2)
                    if isinstance(n, int) and n == M_ITERS - 1 and (job, bank) == (10, 3):
                        merged_low(8, 12, 3)
                        merged_low(12, 14, 4)

            def merged_low(lo, hi, ready):
                dve.wait_ge(merged_hi_ready, ready)
                nc.vector.tensor_tensor(x_lo[:, lo:hi, :], merged[:, lo:hi, :], x_hi[:, lo:hi, :].bitcast(F32),
                                        ALU.subtract).then_inc(merged_lo_ready, 1)

            def iter_o(n, last_iter):
                for r in range(NR):
                    dve.wait_ge(full[r], fills_o(r, n) + 1)
                    if isinstance(n, int) and n == 0:
                        dve.wait_ge(x_in[r], 16)
                    chunk = z[:, r, bass.ds(n * SEQ, SEQ)]
                    nc.vector.scalar_tensor_tensor(chunk, chunk, ALPHA, acc[r][:], ALU.mult, ALU.add)\
                        .then_inc(free[r], 1)
                    dve.wait_ge(free[r], fills_o(r, n) + 1)
                    nc.vector.bn_stats(stats[:, r, bass.ds(n, 1), :].rearrange("p n s -> p (n s)"), chunk)\
                        .then_inc(stats_ready, 1)
                    if not last_iter:
                        continue
                    dve.wait_ge(stats_ready, NR * n + r + 1)
                    nc.vector.bn_aggr(meanvar[:, r, :], stats[:, r, :, :].rearrange("p n s -> p (n s)"))\
                        .then_inc(ln_step, 1)
                    dve.wait_ge(ln_step, 6 * r + 1)
                    var, inv, cor = variance[:, r:r + 1], rstd[:, r:r + 1], correction[:, r:r + 1]
                    nc.vector.tensor_scalar(var, meanvar[:, r, 1:2], EPS, None, ALU.add).then_inc(var_ready, 1)
                    dve.wait_ge(root_ready, r + 1)
                    nc.vector.reciprocal(inv, root[:, r:r + 1]).then_inc(ln_step, 1)
                    dve.wait_ge(ln_step, 6 * r + 2)
                    nc.vector.tensor_scalar(cor, inv, inv, var, ALU.mult, ALU.mult).then_inc(ln_step, 1)
                    dve.wait_ge(ln_step, 6 * r + 3)
                    nc.vector.tensor_scalar(cor, cor, -0.5, 1.5, ALU.mult, ALU.add).then_inc(ln_step, 1)
                    dve.wait_ge(ln_step, 6 * r + 4)
                    nc.vector.tensor_scalar(inv, inv, cor, None, ALU.mult).then_inc(ln_step, 1)
                    dve.wait_ge(ln_step, 6 * r + 5)
                    nc.vector.tensor_scalar(shift[:, r:r + 1], meanvar[:, r, 0:1], inv, -1.0,
                                            ALU.mult, ALU.mult).then_inc(ln_step, 1)
                    if r == 0:
                        dve.wait_ge(row_in, 32)
                    width = LN_SPLIT[r] // LN_PARTS[r]
                    for part in range(LN_PARTS[r]):
                        c = slice(width * part, width * (part + 1))
                        nc.vector.scalar_tensor_tensor(z[:, r, c], z[:, r, c], meanvar[:, r, 0:1], g_row[:, c],
                                                       ALU.subtract, ALU.mult).then_inc(scaled, 1)
                        dve.wait_ge(scaled, 2 * (r + part) + 1)
                        nc.vector.scalar_tensor_tensor(z[:, r, c], z[:, r, c], inv, b_row[:, c],
                                                       ALU.mult, ALU.add).then_inc(scaled, 1)

            iter_a(0, False)
            with dve.Fori(1, A_ITERS) as i:
                iter_a(i, True)
            dve.wait_ge(table_done, 4)
            iter_b(0, True)
            with dve.Fori(1, B_HEADS) as h:
                iter_b(h, False)
            iter_m(0, True)
            with dve.Fori(1, M_ITERS - 1) as n:
                iter_m(n, False)
            iter_m(M_ITERS - 1, False)
            merged_low(14, 16, 5)
            iter_o(0, False)
            with dve.Fori(1, O_ITERS - 1) as n:
                iter_o(n, False)
            iter_o(O_ITERS - 1, True)

        @block.tensor
        def _(pe):
            started = [False]

            def products(into, is_full, pairs, cols, start, stop, released):
                n = 3 * len(pairs)
                k = 0
                for s_hi, s_lo, m_hi, m_lo in pairs:
                    for s, m in ((s_hi, m_hi), (s_hi, m_lo), (s_lo, m_hi)):
                        ins = nc.tensor.matmul(into[:, 0:cols], s, m, start=start and k == 0, stop=stop and k == n - 1)
                        if k == 0 and released and started[0]:
                            ins.then_inc(slot_used, 1)
                        started[0] = True
                        k += 1
                if stop:
                    ins.then_inc(is_full, 1)

            def x_moving(k):
                return x_hi[:, k, :], x_lo[:, k, :]

            def scores_a(u):
                b, j = divmod(u, 2)
                lo = P if b == 0 else 0
                keys = slice((b - 1) * P + lo, (b + 1) * P)
                for hh in range(2):
                    for k in (k_hi_a, k_lo_a):
                        last = nc.tensor.matmul(ps_scores[:, hh * SEQ + lo:hh * SEQ + 2 * P],
                                                q_split[:, 2 * j + hh, b * P:b * P + P], k[:, j, keys],
                                                start=k is k_hi_a, stop=k is k_lo_a)
                last.then_inc(scores_ready, 1)

            def scores_b(u):
                q = slice(u * P, u * P + P)
                nc.tensor.matmul(ps_scores[:, 0:SEQ], q_b[:, 0, q], k_b[:, 0, :], start=True, stop=True)
                nc.tensor.matmul(ps_scores[:, SEQ:SEQ + P], q_b[:, 1, q], k_b[:, 1, q], start=True, stop=True)
                nc.tensor.matmul(ps_scores[:, SEQ + P:SEQ + 2 * P], q_b[:, 2, q], k_b[:, 2, q], start=True, stop=True)\
                    .then_inc(scores_ready, 1)

            def attend(kind, plan, g, first_unit, i):
                for stage, u in plan.get(g, ()):
                    a = first_unit + u
                    if stage == "scores":
                        if kind == "a":
                            if u < 2:
                                pe.wait_ge(q_ready, i * 4 + (2 * u + 2))
                            if u:
                                pe.wait_ge(negmax_ready, a)
                            scores_a(u)
                        else:
                            if u == 0:
                                pe.wait_ge(rope_done, ropes_b(i, 6))
                            pe.wait_ge(negmax_ready, a)
                            pe.wait_ge(probsT_rest, a)
                            scores_b(u)
                    elif stage == "turn_probs":
                        pe.wait_ge(normalised, a + 1)
                        if kind == "b" or u:
                            pe.wait_ge(probsT_ready, a)
                            pe.wait_ge(probsT_rest, a)
                        if kind == "a":
                            b, j = divmod(u, 2)
                            for hh in range(2):
                                for kb in ((1,) if b == 0 else (0, 1)):
                                    c = (2 * kb + hh) * P
                                    last = nc.tensor.transpose(ps_turn[:, c:c + P], probs_a[:, j, hh, kb * P:kb * P + P],
                                                               ident[:])
                        else:
                            for c in range(6):
                                dst = ps_turn[:, c * P:c * P + P] if c < 4 else ps_scores[:, (c + 2) * P:(c + 3) * P]
                                last = nc.tensor.transpose(dst, probs_b[:, c * P:c * P + P], ident[:])
                        last.then_inc(probsT_psum, 1)
                    elif stage == "values":
                        pe.wait_ge(probsT_ready, a + 1)
                        pe.wait_ge(probsT_rest, a + 1)
                        if kind == "b" or u:
                            pe.wait_ge(out_gated, a)
                        if kind == "a":
                            b, j = divmod(u, 2)
                            kbs = (1,) if b == 0 else (0, 1)
                            for kb in kbs:
                                for n, (v, p) in enumerate(((v_hi_a, probsT_hi), (v_hi_a, probsT_lo), (v_lo_a, probsT_hi))):
                                    last = nc.tensor.matmul(ps_out[:, 0:2 * P], v[:, b - 1 + kb, j, :],
                                                            p[:, 2 * kb:2 * kb + 2, :].rearrange("p c q -> p (c q)"),
                                                            start=kb == kbs[0] and n == 0, stop=kb == 1 and n == 2)
                        else:
                            if u == 0:
                                for bank in range(4):
                                    pe.wait_ge(free[bank], fills_b(bank, i + 1))
                            for c in range(6):
                                tile, grp = (c, 0) if c < 4 else (u, c - 3)
                                last = nc.tensor.matmul(ps_out[:, 0:P], v_b[:, tile, grp * P:grp * P + P], probsT[:, c, :],
                                                        start=c == 0, stop=c == 5)
                        last.then_inc(out_psum, 1)

            pe.wait_ge(ident_step, 2)
            for _ in range(WARM_UP):
                nc.tensor.transpose(ps_turn[:, 0:P], ident[:], ident[:])

            for e in range(8):
                m = e // 2
                if e % 2 == 0:
                    pe.wait_ge(lo_done, m + 1)
                pe.wait_ge(x_lo_done, e + 1)
                for t, bank in enumerate((ps_scores[:, 0:SEQ], ps_out[:])):
                    pairs = []
                    for k in range(2):
                        c = slice(256 * (2 * (e % 2) + k) + P * t, 256 * (2 * (e % 2) + k) + P * t + P)
                        pairs.append((w_hi[:, m, c], w_lo[:, m, c], *x_moving(2 * e + k)))
                    products(bank, kv_full, pairs, SEQ, e == 0, e == 7, t == 0 and e % 2 == 0)

            def ready(n, off):
                pe.wait_ge(lo_done, n + (off + 1 - PRO_JOBS + 4))

            def iter_a(i, with_attention):
                for g, (job, _, q, bank, first, last, opens, released) in enumerate(A_BLOCKS):
                    if with_attention:
                        attend("a", A_PLAN, g, unit_a(i - 1), i - 1)
                    elif g == 8:
                        pe.wait_ge(v_out, 1)
                        pe.wait_ge(ident_step, 2)
                        for b in range(4):
                            t = nc.tensor.transpose(ps_turn[:, b * P:b * P + P], vT_a[:, b * P:b * P + P], ident[:])
                        t.then_inc(v_turned, 1)
                    if opens:
                        ready(job_a(i), job)
                    if first and with_attention:
                        pe.wait_ge(free[bank], fills_a(bank, i))
                    s, (half, j) = job % RING, divmod(bank, 2)
                    pairs = []
                    for k in range(2):
                        c = 512 * half + 256 * k + P * j
                        pairs.append((w_hi[:, s, c:c + P], w_lo[:, s, c:c + P], *x_moving(2 * q + k)))
                    products(acc[bank], full[bank], pairs, SEQ, first, last, released)

            def iter_b(h, first_iter):
                for g, (job, group, q, bank, first, last, opens, released) in enumerate(B_BLOCKS):
                    if first_iter:
                        attend("a", A_PLAN, g, unit_a(A_ITERS - 1), A_ITERS - 1)
                    else:
                        attend("b", B_PLAN, g, unit_b(h - 1), h - 1)
                    if opens:
                        ready(job_b(h), job)
                    if first:
                        pe.wait_ge(free[bank], fills_b(bank, h) + (group - (1 if bank == 3 else 0)))
                    s = job % RING
                    pairs = []
                    for k in range(2):
                        if group == 2:
                            c, r = slice(384 * k, 384 * k + 384), slice(bank * P, bank * P + P)
                            kk = 2 * q + k
                            pairs.append((x_hi[:, kk, r], x_lo[:, kk, r], w_hi[:, s, c], w_lo[:, s, c]))
                        else:
                            c = (384, 512)[group] * k + bank * P
                            pairs.append((w_hi[:, s, c:c + P], w_lo[:, s, c:c + P], *x_moving(2 * q + k)))
                    products(acc[bank], full[bank], pairs, 384 if group == 2 else SEQ, first, last, released)

            def iter_m(n, first_iter):
                for g, (job, group, q, bank, first, last, opens, released) in enumerate(M_BLOCKS):
                    if first_iter:
                        attend("b", B_PLAN_MERGE, g, unit_b(B_HEADS - 1), B_HEADS - 1)
                    if opens:
                        ready(job_m(n), job)
                    if first:
                        pe.wait_ge(free[bank], fills_m(bank, n) + group // 2)
                        if first_iter and bank % 2 == 0 and group >= 2:
                            pe.wait_ge(og_ready, (8, 12)[group - 2])
                    s, t = job % RING, bank % 2
                    pairs = []
                    for k in range(4 if group < 3 else 2):
                        c = slice(256 * k + P * t, 256 * k + P * t + P)
                        if group < 2:
                            moving = x_moving(4 * q + k)
                        else:
                            e = 4 * q + k if group == 2 else 8 + 2 * q + k
                            moving = og_hi[:, e, :], og_lo[:, e, :]
                        pairs.append((w_hi[:, s, c], w_lo[:, s, c], *moving))
                    products(acc[bank], full[bank], pairs, SEQ, first, last, released)

            def iter_o(n, first_iter, last_iter):
                for job, _, q, bank, first, last, opens, released in (O_BLOCKS_LAST if last_iter else O_BLOCKS):
                    if opens:
                        ready(job_o(n), job)
                        if first_iter:
                            pe.wait_ge(merged_lo_ready, (1, 1, 2, 2, 3, 3, 4, 5)[q])
                    if first:
                        pe.wait_ge(free[bank], fills_o(bank, n))
                    s, r = job % RING, slice(bank * P, bank * P + P)
                    pairs = [(x_hi[:, 2 * q + k, r], x_lo[:, 2 * q + k, r], w_hi[:, s, 512 * k:512 * k + 512],
                              w_lo[:, s, 512 * k:512 * k + 512]) for k in range(2)]
                    products(acc[bank], full[bank], pairs, SEQ, first, last, released)

            iter_a(0, False)
            pe.wait_ge(v_a_ready, 1)
            pe.wait_ge(k_split, 8)
            with pe.Fori(1, A_ITERS) as i:
                iter_a(i, True)
            iter_b(0, True)
            with pe.Fori(1, B_HEADS) as h:
                iter_b(h, False)
            iter_m(0, True)
            with pe.Fori(1, M_ITERS) as n:
                iter_m(n, False)
            iter_o(0, True, False)
            with pe.Fori(1, O_ITERS - 1) as n:
                iter_o(n, False, False)
            iter_o(O_ITERS - 1, False, True)


def kernel(x, positions, w_in, b_gate, sinks, w_pa, w_pb, w_out, ln_g, ln_b):
    import numpy as np
    import concourse.bacc as bacc
    from concourse.bass_utils import run_bass_kernel_spmd

    x, positions, w_in, b_gate, sinks, w_pa, w_pb, w_out, ln_g, ln_b = (
        np.asarray(a) for a in (x, positions, w_in, b_gate, sinks, w_pa, w_pb, w_out, ln_g, ln_b))
    t = (4 * np.arange(P)[None, :] + np.arange(NR)[:, None]).reshape(-1)

    p = np.arange(P)
    rope_rows = np.stack([10000.0 ** (-(p % 64) / 64.0), np.where(p < 64, -1.0, 1.0),
                          10000.0 ** (-(p % 32) / 32.0), np.where(p % 64 < 32, -1.0, 1.0)], axis=1).astype(np.float32)
    in_block = (4 * np.arange(32)[None, :] + np.arange(NR)[:, None]).reshape(-1)
    dist = in_block[:, None] - np.concatenate([in_block - P, in_block])[None, :]
    mask_a = np.where((dist >= 0) & (dist < 128), 0.0, MASKED).astype(np.float32)
    far = t.reshape(NR, P)[:, :, None] - t[None, None, :]
    near = np.where((far >= 0) & (far <= 128), 0.0, MASKED).transpose(1, 0, 2).reshape(P, NR * SEQ)
    step = p[:, None] - p[None, :]
    by4 = np.where(step >= 0, 0.0, MASKED)
    by16 = np.where((step >= 0) & (step % 4 == 0), 0.0, MASKED)
    mask_b = np.concatenate([near, by4, by16], axis=1).astype(np.float32)

    arrays = {
        "xT": np.ascontiguousarray(x[0].T[:, t]),
        "x": x[0],
        "pos": np.ascontiguousarray(positions[0][t]),
        "w_in": w_in[0],
        "gate_bias": np.ascontiguousarray(b_gate[0].reshape(2 * KT, P).T),
        "sinks": np.ascontiguousarray(sinks[0].reshape(A_KV, A_ITERS, 2).transpose(1, 0, 2).reshape(A_HEADS)),
        "w_pa": w_pa[0], "w_pb": w_pb[0], "w_out": w_out[0], "ln_g": ln_g[0], "ln_b": ln_b[0],
        "rope_rows": rope_rows, "mask_a": mask_a, "mask_b": mask_b,
    }
    nc = bacc.Bacc("TRN2", target_bir_lowering=False, num_devices=1)
    args = [nc.dram_tensor(n, a.shape, mybir.dt.from_np(a.dtype), kind="ExternalInput").ap() for n, a in arrays.items()]
    out = nc.dram_tensor("out", (1, SEQ, D), F32, kind="ExternalOutput").ap()
    build(nc, *args, out)
    run = run_bass_kernel_spmd(nc, [arrays], core_ids=[0])
    return run.results[0]["out"]
```
